# Optimizing a Trainium2 kernel written in Bass

```python
import jax, jax.numpy as jnp
from jax import lax
import numpy as np

D_MODEL = 1024
BATCH = 1
SEQ = 256
DEPTH = 2

CHUNK = 64
SB_BLOCK = 128
EPS = 1e-6
GLA_HEADS = 4
GLA_HEAD_K = 64
GLA_HEAD_V = 128
GLA_DK = GLA_HEADS * GLA_HEAD_K
GLA_DV = GLA_HEADS * GLA_HEAD_V
GLA_GATE_RANK = 16
GLA_GATE_NORMALIZER = 16.0
SB_HEADS = 8
SB_HEAD_DIM = 64
SB_D = SB_HEADS * SB_HEAD_DIM
MIX_WIDTH = GLA_DV + SB_D
IN_WIDTH = 2 * GLA_DK + 2 * GLA_DV + GLA_GATE_RANK + 3 * SB_D
CONV_WIDTH = 31
D_FF = -(-8 * D_MODEL // (3 * 256)) * 256
N_EVEN = (DEPTH + 1) // 2
N_ODD = DEPTH // 2


def _rms_f32(xf, g):
    return xf * lax.rsqrt(jnp.mean(xf * xf, axis=-1, keepdims=True) + EPS) * g.astype(jnp.float32)

def rms_norm(x, g):
    return _rms_f32(x.astype(jnp.float32), g).astype(x.dtype)

def gla_mixer(q, k, v, r, gate_lr, w_gate2, b_gate, g_out):
    f32 = jnp.float32
    B, T, _ = q.shape
    nc = T // CHUNK
    log_a = jax.nn.log_sigmoid((gate_lr @ w_gate2 + b_gate).astype(f32)) / GLA_GATE_NORMALIZER

    def split(t, hd):
        return t.astype(f32).reshape(B, nc, CHUNK, -1, hd).transpose(0, 3, 1, 2, 4)

    qc = split(q, GLA_HEAD_K) * (GLA_HEAD_K ** -0.5)
    kc = split(k, GLA_HEAD_K)
    vc = split(v, GLA_HEAD_V)
    bc = jnp.cumsum(split(log_a, GLA_HEAD_K), axis=3)
    b_end = bc[:, :, :, -1:, :]
    k_end = kc * jnp.exp(b_end - bc)
    scores = jnp.einsum('bhnik,bhnjk->bhnij', qc, k_end)
    intra = jnp.einsum('bhnij,bhnjv->bhniv', scores, vc)
    chunk_update = jnp.einsum('bhnjk,bhnjv->bhnkv', k_end, vc)
    chunk_decay = jnp.exp(b_end[:, :, :, 0, :])

    def step(s, inp):
        a, u = inp
        return a[..., None] * s + u, s

    s0 = jnp.zeros((B, GLA_HEADS, GLA_HEAD_K, GLA_HEAD_V), f32)
    _, s_prev = lax.scan(step, s0, (jnp.moveaxis(chunk_decay, 2, 0), jnp.moveaxis(chunk_update, 2, 0)))
    s_prev = jnp.moveaxis(s_prev, 0, 2)
    inter = jnp.einsum('bhnik,bhnkv->bhniv', qc * jnp.exp(b_end), s_prev)
    o = _rms_f32(intra + inter, g_out)
    o = o.transpose(0, 2, 3, 1, 4).reshape(B, T, GLA_DV)
    return o * jax.nn.silu(r.astype(f32))

def stick_breaking_mixer(q, k, v, g_q, g_k):
    f32 = jnp.float32
    B, T, _ = q.shape

    def heads(t):
        return t.astype(f32).reshape(B, T, SB_HEADS, SB_HEAD_DIM).transpose(0, 2, 1, 3)

    qh = _rms_f32(heads(q), g_q) * (SB_HEAD_DIM ** -0.5)
    kh = _rms_f32(heads(k), g_k)
    vh = heads(v)
    outs = []
    for blk in range(T // SB_BLOCK):
        q0 = blk * SB_BLOCK
        kv_len = q0 + SB_BLOCK
        past = np.arange(kv_len)[None, :] < np.arange(q0, kv_len)[:, None]
        z = jnp.einsum('bhtd,bhsd->bhts', qh[:, :, q0:kv_len], kh[:, :, :kv_len])
        log_keep = jnp.where(past, jax.nn.log_sigmoid(-z), 0.0)
        between = lax.cumsum(log_keep, axis=3, reverse=True) - log_keep
        w = jnp.where(past, jnp.exp(jax.nn.log_sigmoid(z) + between), 0.0)
        outs.append(jnp.einsum('bhts,bhsd->bhtd', w, vh[:, :, :kv_len]))
    o = jnp.concatenate(outs, axis=2)
    return o.transpose(0, 2, 1, 3).reshape(B, T, SB_D)

def hybrid_mixer(h, w_in, w_gate2, b_gate, g_gla, g_q, g_k, w_out):
    proj = h @ w_in
    cuts = np.cumsum([GLA_DK, GLA_DK, GLA_DV, GLA_DV, GLA_GATE_RANK, SB_D, SB_D])
    gq, gk, gv, gr, glr, sq, sk, sv = jnp.split(proj, cuts, axis=-1)
    o_gla = gla_mixer(gq, gk, gv, gr, glr, w_gate2, b_gate, g_gla)
    o_sb = stick_breaking_mixer(sq, sk, sv, g_q, g_k)
    o = jnp.concatenate([o_gla, o_sb], axis=-1).astype(h.dtype)
    return o @ w_out

def conformer_conv(h, w_pw1, b_pw1, w_dw, b_dw, ln_g, ln_b, w_pw2, b_pw2):
    a = h @ w_pw1 + b_pw1
    u = a[..., :D_MODEL] * jax.nn.sigmoid(a[..., D_MODEL:])
    u = lax.conv_general_dilated(u, w_dw[:, None, :].astype(u.dtype), window_strides=(1,),
                                 padding=[(CONV_WIDTH - 1, 0)],
                                 dimension_numbers=('NWC', 'WIO', 'NWC'),
                                 feature_group_count=D_MODEL) + b_dw
    uf = u.astype(jnp.float32)
    mu = jnp.mean(uf, axis=-1, keepdims=True)
    var = jnp.mean(jnp.square(uf - mu), axis=-1, keepdims=True)
    u = ((uf - mu) * lax.rsqrt(var + EPS) * ln_g + ln_b).astype(h.dtype)
    return jax.nn.silu(u) @ w_pw2 + b_pw2

def swiglu(h, wg, wu, wd):
    return (jax.nn.silu(h @ wg) * (h @ wu)) @ wd

def first_inputs(seed: int = 0) -> dict:
    key = jax.random.key(seed)
    ks = iter(jax.random.split(key, 32))

    def nrm(shape, scale):
        return jax.random.normal(next(ks), shape, jnp.float32) * scale

    def gain(shape):
        return 1.0 + nrm(shape, 0.05)

    return {
        "x": nrm((BATCH, SEQ, D_MODEL), 1.0),
        "mix_norm": gain((DEPTH, D_MODEL)),
        "ffn_norm": gain((DEPTH, D_MODEL)),
        "hy_w_in": nrm((N_EVEN, D_MODEL, IN_WIDTH), D_MODEL ** -0.5),
        "hy_w_gate2": nrm((N_EVEN, GLA_GATE_RANK, GLA_DK), GLA_GATE_RANK ** -0.5),
        "hy_b_gate": nrm((N_EVEN, GLA_DK), 0.1),
        "hy_gla_norm": gain((N_EVEN, GLA_HEAD_V)),
        "hy_sb_q_norm": gain((N_EVEN, SB_HEAD_DIM)),
        "hy_sb_k_norm": gain((N_EVEN, SB_HEAD_DIM)),
        "hy_w_out": nrm((N_EVEN, MIX_WIDTH, D_MODEL), MIX_WIDTH ** -0.5),
        "cv_w_pw1": nrm((N_ODD, D_MODEL, 2 * D_MODEL), D_MODEL ** -0.5),
        "cv_b_pw1": nrm((N_ODD, 2 * D_MODEL), 0.02),
        "cv_w_dw": nrm((N_ODD, CONV_WIDTH, D_MODEL), CONV_WIDTH ** -0.5),
        "cv_b_dw": nrm((N_ODD, D_MODEL), 0.02),
        "cv_ln_g": gain((N_ODD, D_MODEL)),
        "cv_ln_b": nrm((N_ODD, D_MODEL), 0.02),
        "cv_w_pw2": nrm((N_ODD, D_MODEL, D_MODEL), D_MODEL ** -0.5),
        "cv_b_pw2": nrm((N_ODD, D_MODEL), 0.02),
        "ffn_w_gate": nrm((DEPTH, D_MODEL, D_FF), D_MODEL ** -0.5),
        "ffn_w_up": nrm((DEPTH, D_MODEL, D_FF), D_MODEL ** -0.5),
        "ffn_w_down": nrm((DEPTH, D_FF, D_MODEL), D_FF ** -0.5),
    }

def first_block(x, mix_norm, ffn_norm, hy_w_in, hy_w_gate2, hy_b_gate, hy_gla_norm,
              hy_sb_q_norm, hy_sb_k_norm, hy_w_out, cv_w_pw1, cv_b_pw1, cv_w_dw, cv_b_dw,
              cv_ln_g, cv_ln_b, cv_w_pw2, cv_b_pw2, ffn_w_gate, ffn_w_up, ffn_w_down):
    h = x
    for layer in range(DEPTH):
        hn = rms_norm(h, mix_norm[layer])
        if layer % 2 == 0:
            i = layer // 2
            mix = hybrid_mixer(hn, hy_w_in[i], hy_w_gate2[i], hy_b_gate[i], hy_gla_norm[i],
                               hy_sb_q_norm[i], hy_sb_k_norm[i], hy_w_out[i])
        else:
            i = layer // 2
            mix = conformer_conv(hn, cv_w_pw1[i], cv_b_pw1[i], cv_w_dw[i], cv_b_dw[i],
                                 cv_ln_g[i], cv_ln_b[i], cv_w_pw2[i], cv_b_pw2[i])
        h = h + mix.astype(h.dtype)
        h = h + swiglu(rms_norm(h, ffn_norm[layer]), ffn_w_gate[layer], ffn_w_up[layer],
                       ffn_w_down[layer]).astype(h.dtype)
    return h


DEPTH_2 = 1

RET_HEADS = 4
RET_QK_DIM = 256
RET_V_DIM = 256
RET_QK = RET_HEADS * RET_QK_DIM
RET_V = RET_HEADS * RET_V_DIM
POOL_WINDOWS = (2, 4, 8, 16)
POOL_GROUPS = 4
POOL_GROUP_DIM = 256
POOL_WIDTH = POOL_GROUPS * POOL_GROUP_DIM
N_BRANCH = 2
IN_WIDTH_2 = 2 * RET_QK + 2 * RET_V + POOL_WIDTH + N_BRANCH * D_MODEL
D_FF_2 = 2816
ROPE_BASE = 10000.0
NORM_EPS = 1e-6
FFN_RES_WEIGHT = 0.5


def rmsnorm(x, g):
    xf = x.astype(jnp.float32)
    y = xf * lax.rsqrt(jnp.mean(xf * xf, axis=-1, keepdims=True) + NORM_EPS)
    return (y * g.astype(jnp.float32)).astype(x.dtype)

def swiglu_ffn(x, w_in, w_out):
    gate, up = jnp.split(x @ w_in, 2, axis=-1)
    return (jax.nn.silu(gate) * up) @ w_out

def rotary(x):
    s, d = x.shape[1], x.shape[-1]
    half = d // 2
    inv_freq = ROPE_BASE ** (-jnp.arange(half, dtype=jnp.float32) / half)
    ang = jnp.arange(s, dtype=jnp.float32)[:, None] * inv_freq[None, :]
    cos = jnp.cos(ang)[None, :, None, :].astype(x.dtype)
    sin = jnp.sin(ang)[None, :, None, :].astype(x.dtype)
    x1, x2 = x[..., :half], x[..., half:]
    return jnp.concatenate([x1 * cos - x2 * sin, x1 * sin + x2 * cos], axis=-1)

def retention(q, k, v):
    b, s, h, dk = q.shape
    dv = v.shape[-1]
    nc = s // CHUNK
    log_gamma = jnp.log(1.0 - 2.0 ** (-5.0 - jnp.arange(h, dtype=jnp.float32)))
    idx = jnp.arange(CHUNK, dtype=jnp.float32)
    inner_decay = jnp.exp(log_gamma[:, None, None] * jnp.abs(idx[:, None] - idx[None, :]))
    q_decay = jnp.exp(log_gamma[None, :] * (idx[:, None] + 1.0))
    k_decay = jnp.exp(log_gamma[None, :] * (CHUNK - 1.0 - idx[:, None]))
    chunk_decay = jnp.exp(log_gamma * CHUNK)

    qc = q.reshape(b, nc, CHUNK, h, dk)
    kc = k.reshape(b, nc, CHUNK, h, dk)
    vc = v.reshape(b, nc, CHUNK, h, dv)

    scores = jnp.einsum("bnchd,bnshd->bnhcs", qc, kc) * inner_decay[None, None]
    inner = jnp.einsum("bnhcs,bnshe->bnche", scores, vc)

    def step(state, inp):
        q_i, k_i, v_i = inp
        cross = jnp.einsum("bchd,bhde->bche", q_i * q_decay[None, :, :, None], state)
        new_state = state * chunk_decay[None, :, None, None] + jnp.einsum(
            "bchd,bche->bhde", k_i * k_decay[None, :, :, None], v_i)
        return new_state, cross

    state0 = jnp.zeros((b, h, dk, dv), jnp.float32)
    xs = (qc.transpose(1, 0, 2, 3, 4), kc.transpose(1, 0, 2, 3, 4), vc.transpose(1, 0, 2, 3, 4))
    _, cross = lax.scan(step, state0, xs)
    out = inner + cross.transpose(1, 0, 2, 3, 4)
    return out.reshape(b, s, h, dv)

def multiscale_pool(p, w_group, scale):
    b, s, _ = p.shape
    pf = p.astype(jnp.float32).reshape(b, s, POOL_GROUPS, POOL_GROUP_DIM)
    cs = jnp.concatenate([jnp.zeros((b, 1, POOL_GROUPS, POOL_GROUP_DIM), jnp.float32),
                          jnp.cumsum(pf, axis=1)], axis=1)
    t = jnp.arange(s, dtype=jnp.float32)
    outs = []
    for g, w in enumerate(POOL_WINDOWS):
        cs_g = cs[:, :, g]
        shifted = jnp.pad(cs_g[:, : s + 1 - w], ((0, 0), (w - 1, 0), (0, 0)))
        count = jnp.minimum(t + 1.0, float(w))[None, :, None]
        outs.append((cs_g[:, 1:] - shifted) / count - pf[:, :, g])
    pooled = jnp.stack(outs, axis=2)
    mixed = jnp.einsum("bsgc,gcd->bsgd", pooled, w_group.astype(jnp.float32))
    return (mixed.reshape(b, s, POOL_WIDTH) * scale.astype(jnp.float32)).astype(p.dtype)

def second_inputs(seed: int = 0) -> dict:
    key = jax.random.key(seed)
    ks = jax.random.split(key, 20)
    f32 = jnp.float32

    def nrm(k, shape, fan_in):
        return jax.random.normal(k, shape, f32) * (fan_in ** -0.5)

    def gain(k, shape):
        return 1.0 + 0.02 * jax.random.normal(k, shape, f32)

    return {
        "x": jax.random.normal(ks[0], (BATCH, SEQ, D_MODEL), f32),
        "norm_ffn1": gain(ks[1], (DEPTH_2, D_MODEL)),
        "ffn1_w_in": nrm(ks[2], (DEPTH_2, D_MODEL, 2 * D_FF_2), D_MODEL),
        "ffn1_w_out": nrm(ks[3], (DEPTH_2, D_FF_2, D_MODEL), D_FF_2),
        "norm_mix": gain(ks[4], (DEPTH_2, D_MODEL)),
        "w_in": nrm(ks[5], (DEPTH_2, D_MODEL, IN_WIDTH_2), D_MODEL),
        "gate_bias": 0.02 * jax.random.normal(ks[6], (DEPTH_2, N_BRANCH, D_MODEL), f32),
        "pool_w": nrm(ks[7], (DEPTH_2, POOL_GROUPS, POOL_GROUP_DIM, POOL_GROUP_DIM), POOL_GROUP_DIM),
        "pool_scale": gain(ks[8], (DEPTH_2, POOL_WIDTH)),
        "w_ret_up": nrm(ks[9], (DEPTH_2, RET_V, D_MODEL), RET_V),
        "w_pool_up": nrm(ks[10], (DEPTH_2, POOL_WIDTH, D_MODEL), POOL_WIDTH),
        "w_out": nrm(ks[11], (DEPTH_2, D_MODEL, D_MODEL), D_MODEL),
        "norm_ffn2": gain(ks[12], (DEPTH_2, D_MODEL)),
        "ffn2_w_in": nrm(ks[13], (DEPTH_2, D_MODEL, 2 * D_FF_2), D_MODEL),
        "ffn2_w_out": nrm(ks[14], (DEPTH_2, D_FF_2, D_MODEL), D_FF_2),
        "norm_final": gain(ks[15], (D_MODEL,)),
    }

def second_block(x, norm_ffn1, ffn1_w_in, ffn1_w_out, norm_mix, w_in, gate_bias, pool_w,
              pool_scale, w_ret_up, w_pool_up, w_out, norm_ffn2, ffn2_w_in, ffn2_w_out,
              norm_final):
    b, s, _ = x.shape
    split_points = [RET_QK, 2 * RET_QK, 2 * RET_QK + RET_V, 2 * RET_QK + 2 * RET_V,
                    2 * RET_QK + 2 * RET_V + POOL_WIDTH]
    h = x
    for l in range(DEPTH_2):
        h = h + FFN_RES_WEIGHT * swiglu_ffn(rmsnorm(h, norm_ffn1[l]), ffn1_w_in[l], ffn1_w_out[l])

        u = rmsnorm(h, norm_mix[l])
        proj = u @ w_in[l]
        q, k, v, g_ret, p, gates = jnp.split(proj, split_points, axis=-1)
        q = rotary(q.reshape(b, s, RET_HEADS, RET_QK_DIM))
        k = rotary(k.reshape(b, s, RET_HEADS, RET_QK_DIM)) * (RET_QK_DIM ** -0.5)
        v = v.reshape(b, s, RET_HEADS, RET_V_DIM)
        ret = retention(q.astype(jnp.float32), k.astype(jnp.float32), v.astype(jnp.float32))
        ret = ret * lax.rsqrt(jnp.mean(ret * ret, axis=-1, keepdims=True) + NORM_EPS)
        ret = ret.reshape(b, s, RET_V).astype(proj.dtype) * jax.nn.silu(g_ret)

        pool_out = multiscale_pool(p, pool_w[l], pool_scale[l])

        gate = jax.nn.sigmoid(gates.reshape(b, s, N_BRANCH, D_MODEL) + gate_bias[l])
        merged = gate[:, :, 0] * (ret @ w_ret_up[l]) + gate[:, :, 1] * (pool_out @ w_pool_up[l])
        h = h + merged @ w_out[l]

        h = h + FFN_RES_WEIGHT * swiglu_ffn(rmsnorm(h, norm_ffn2[l]), ffn2_w_in[l], ffn2_w_out[l])
    return rmsnorm(h, norm_final)


def setup_inputs(seed=0):
    out = dict(first_inputs(seed))
    for name, value in second_inputs(seed + 1).items():
        if name != "x":
            out[name + "_2"] = value
    return out


def reference(
    x, mix_norm, ffn_norm, hy_w_in, hy_w_gate2, hy_b_gate, hy_gla_norm, hy_sb_q_norm,
    hy_sb_k_norm, hy_w_out, cv_w_pw1, cv_b_pw1, cv_w_dw, cv_b_dw, cv_ln_g, cv_ln_b, cv_w_pw2,
    cv_b_pw2, ffn_w_gate, ffn_w_up, ffn_w_down, norm_ffn1_2, ffn1_w_in_2, ffn1_w_out_2,
    norm_mix_2, w_in_2, gate_bias_2, pool_w_2, pool_scale_2, w_ret_up_2, w_pool_up_2, w_out_2,
    norm_ffn2_2, ffn2_w_in_2, ffn2_w_out_2, norm_final_2,
):
    x = first_block(
        x, mix_norm, ffn_norm, hy_w_in, hy_w_gate2, hy_b_gate, hy_gla_norm, hy_sb_q_norm,
        hy_sb_k_norm, hy_w_out, cv_w_pw1, cv_b_pw1, cv_w_dw, cv_b_dw, cv_ln_g, cv_ln_b,
        cv_w_pw2, cv_b_pw2, ffn_w_gate, ffn_w_up, ffn_w_down,
    )
    return second_block(
        x, norm_ffn1_2, ffn1_w_in_2, ffn1_w_out_2, norm_mix_2, w_in_2, gate_bias_2, pool_w_2,
        pool_scale_2, w_ret_up_2, w_pool_up_2, w_out_2, norm_ffn2_2, ffn2_w_in_2, ffn2_w_out_2,
        norm_final_2,
    )


_drawn_inputs = setup_inputs


def setup_inputs(seed=0):
    import zlib

    import numpy as np

    out = dict(_drawn_inputs(seed))
    spreads = {}
    factors = {'hy_sb_q_norm': 4.607,
     'hy_sb_k_norm': 5.044,
     'cv_b_pw1': 5.343,
     'cv_ln_b': 5.667,
     'cv_b_pw2': 3.514,
     'norm_ffn1_2': 8.0,
     'norm_mix_2': 5.706,
     'gate_bias_2': 8.0,
     'pool_scale_2': 25.351,
     'norm_ffn2_2': 29.088,
     'norm_final_2': 8.269}
    for name, (base, spread) in spreads.items():
        noise = np.random.default_rng([zlib.crc32(name.encode()), seed]).standard_normal(out[name].shape)
        drawn = base * np.exp(spread * noise) if base else spread * noise
        out[name] = __import__('jax').numpy.asarray(drawn.astype(out[name].dtype))
    for name, factor in factors.items():
        out[name] = (out[name] * factor).astype(out[name].dtype)
    return out
```

```python
from contextlib import ExitStack

import concourse.bass as bass
from concourse import mybir

P = 128
D = 1024
T = 256
FC = 11
UC = 2048
R = 4
S = 4

F32 = mybir.dt.float32
F32R = mybir.dt.float32r
ALU = mybir.AluOpType
ACT = mybir.ActivationFunctionType
AXX = mybir.AxisListType.X

EPS = 1e-6
NK = {"ident": 0, "later": 128, "ones": 256, "mask": 384, "rest": 640, "blk": 768}
NKW = 770
PAR = {"mix0": 0, "ffn0": 8, "mix1": 16, "ffn1": 24, "n1": 32, "nm": 40, "n2": 48, "gla": 56, "gq": 57, "gk": 58,
       "b_dw": 59, "ln_g": 67, "ln_b": 75, "pool": 83, "w_dw": 91}
PARW = 91 + 8 * 31
UNITS = {"sq": 2, "sk": 2, "sv": 2, "gqk": 2, "gv": 2, "gr": 2, "hout": 4, "ff0": 33, "pw1": 8, "pw2": 4, "ff1": 33,
         "ffa": 33, "p": 4, "pw": 1, "gp": 8, "q": 4, "k": 4, "v": 4, "gret": 4, "gu": 8, "out2": 4, "ffb": 33}


def build(nc, xin, wst, wg, wg2, cst, par, brow, cosin, rmask, pmat, out):
    NU = wst.shape[0]
    assert NU == sum(UNITS.values())
    with ExitStack() as ctx:
        def sb(name, shape, dt=F32):
            return ctx.enter_context(nc.sbuf_tensor(name, shape, dt))

        class Engine:

            def __init__(self, name):
                self.name, self.items, self.count, self.seen = name, [], 0, {}
                self.sem = ctx.enter_context(nc.semaphore("done_" + name))

            def wait(self, *tokens):
                for tok in tokens:
                    if tok is None:
                        continue
                    if isinstance(tok, list):
                        self.wait(*tok)
                        continue
                    sem, value = tok
                    if self.seen.get(sem.name, 0) < value:
                        self.seen[sem.name] = value
                        self.items.append(lambda e, sem=sem, value=value: e.wait_ge(sem, value))

            def do(self, fn, *tokens, inc=True):
                self.wait(*tokens)
                if not inc:
                    self.items.append(fn)
                    return None
                self.count += 1
                self.items.append(lambda e: fn(e).then_inc(self.sem, 1))
                return self.sem, self.count

        pe, act, dve, pool, sp = Engine("pe"), Engine("act"), Engine("dve"), Engine("pool"), Engine("sp")

        raw = sb("raw", [P, R, UC])
        whi = sb("whi", [P, S, UC], F32R)
        wlo = sb("wlo", [P, S, UC], F32R)
        xh = sb("xh", [P, 8, T], F32R)
        xl = sb("xl", [P, 8, T], F32R)
        yh = sb("yh", [P, 8, T], F32R)
        yl = sb("yl", [P, 8, T], F32R)
        h = sb("h", [P, 2, D])
        kc = sb("kc", [P, NKW])
        pr = sb("pr", [P, PARW])
        st = sb("st", [P, 96])
        sil = sb("sil", [P, 2, T])
        hid = sb("hid", [P, 2, T])
        AR = sb("AR", [P, 14080])
        ps = [ctx.enter_context(nc.psum_tensor(f"ps{i}", [P, 512], F32)) for i in range(8)]
        free = [None] * 8

        def const(name, n=P):
            return kc[:, NK[name]:NK[name] + n]

        def parm(name, k=0, n=1):
            return pr[:, PAR[name] + k:PAR[name] + k + n]

        ident = const("ident")

        slot_sem = [ctx.enter_context(nc.semaphore(f"raw{i}")) for i in range(R)]

        def load(dst, src, *tokens):
            sem = ctx.enter_context(nc.semaphore(f"load{len(sp.items)}"))
            sp.wait(*tokens)
            sp.items.append(lambda e: e.dma_start(dst, src).then_inc(sem, 16))
            return sem, 16

        hi_done, lo_done, unit_done = {}, {}, {}
        loaded = [0]
        split = [0]

        def load_unit():
            v = loaded[0]
            if v < NU and (v < R or v - R in lo_done):
                sp.wait(lo_done.get(v - R))
                sem = slot_sem[v % R]
                sp.items.append(lambda e: e.dma_start(raw[:, v % R, :], wst[v]).then_inc(sem, 16))
                loaded[0] += 1
                return True
            return False

        def pump():
            while True:
                while load_unit():
                    pass
                v = split[0]
                if v >= NU or v >= loaded[0] or not (v < S or v - S in unit_done):
                    return
                split[0] += 1
                arrived = (slot_sem[v % R], 16 * (v // R + 1))
                hi_done[v] = act.do(lambda e, v=v: e.copy(whi[:, v % S, :], raw[:, v % R, :]),
                                    arrived, unit_done.get(v - S))
                lo_done[v] = dve.do(lambda e, v=v: e.tensor_tensor(wlo[:, v % S, :], raw[:, v % R, :],
                                                                   whi[:, v % S, :].bitcast(F32), ALU.subtract),
                                    hi_done[v], unit_done.get(v - S))

        at = [0]

        def take(n):
            pump()
            us = list(range(at[0], at[0] + n))
            at[0] += n
            for u in us:
                assert u in lo_done
            return us

        def mm3(o, ah, al, bh, bl, start, stop, skip=False, inc=False):
            pe.do(lambda e: e.matmul(o, ah, bh, start=start, stop=False, skip_group_check=skip), inc=False)
            pe.do(lambda e: e.matmul(o, ah, bl, start=False, stop=False, skip_group_check=skip), inc=False)
            return pe.do(lambda e: e.matmul(o, al, bh, start=False, stop=stop, skip_group_check=skip), inc=inc)

        def mm(o, a, b, start=True, stop=True, skip=False, inc=True, deps=()):
            return pe.do(lambda e: e.matmul(o, a, b, start=start, stop=stop, skip_group_check=skip), *deps, inc=inc)

        def tr(o, i, deps=(), inc=True):
            return pe.do(lambda e: e.transpose(o, i, ident[0:i.shape[0], 0:i.shape[0]]), *deps, inc=inc)

        def A(out_, in_, func, *deps, scale=1.0, bias=0.0, accum=None):
            return act.do(lambda e: e.activation(out_, in_, func, bias=bias, scale=scale, accum_out=accum)
                          if accum is not None else e.activation(out_, in_, func, bias=bias, scale=scale), *deps)

        def TT(out_, a, b, op, *deps, eng=dve):
            return eng.do(lambda e: e.tensor_tensor(out_, a, b, op), *deps)

        def TS(out_, a, s1, s2, op0, op1, *deps, eng=dve):
            if op1 is None:
                return eng.do(lambda e: e.tensor_scalar(out_, a, s1, None, op0), *deps)
            return eng.do(lambda e: e.tensor_scalar(out_, a, s1, s2, op0, op1), *deps)

        def STT(out_, a, s, b, op0, op1, *deps):
            return dve.do(lambda e: e.scalar_tensor_tensor(out=out_, in0=a, scalar=s, in1=b, op0=op0, op1=op1), *deps)

        def rsqrt(out_, ss, n, *deps):
            a = TS(out_, ss, 1.0 / n, EPS, ALU.mult, ALU.add, *deps)
            return TT(out_, out_, nhalf[:, 0:out_.shape[1]], ALU.pow, a, nhalf_t, eng=pool)

        flip = [0]

        def tbank():
            flip[0] ^= 1
            return 6 + flip[0]

        def xpose(src, t, dh, dl, gain, ready, freed):
            done = []
            for half in range(2):
                b = tbank()
                for i in range(4):
                    k = 4 * half + i
                    tok = tr(ps[b][:, 128 * i:128 * i + 128], src[:, 128 * k:128 * k + 128],
                             (ready[half], free[b]), inc=i == 3)
                cols = slice(P * t, P * t + P)
                if all(gain(4 * half + i) is None for i in range(4)):
                    src4 = ps[b][:, :].rearrange("p (k c) -> p k c", k=4)
                    hi4, lo4 = (x[:, 4 * half:4 * half + 4, cols] for x in (dh, dl))
                    a = A(hi4, src4, ACT.Copy, tok, freed)
                    d = TT(lo4, src4, hi4.bitcast(F32), ALU.subtract, a)
                else:
                    for i in range(4):
                        k = 4 * half + i
                        a = A(dh[:, k, cols], ps[b][:, 128 * i:128 * i + 128], ACT.Copy, tok, freed, scale=gain(k))
                    for i in range(4):
                        k = 4 * half + i
                        d = STT(dl[:, k, cols], ps[b][:, 128 * i:128 * i + 128], gain(k),
                                dh[:, k, cols].bitcast(F32), ALU.mult, ALU.subtract, a)
                free[b] = d
                done.append(d)
            return done

        nhalf = sb("nhalf", [P, T])
        nhalf_t = pool.do(lambda e: e.memset(nhalf[:, :], -0.5))
        rstd = st[:, 0:2]
        ss = st[:, 2:4]
        x_ready = [[None, None], [None, None]]
        x_used = [None]
        y_used = [None]
        h_ready = [[None, None], [None, None]]
        rstd_ready = [None, None]
        rstd_used = [None, None]
        junk = AR[:, 13056:14080]
        junk_used = [None]

        def norm(t, name):
            x_ready[t] = xpose(h[:, t, :], t, xh, xl, lambda k: parm(name, k), h_ready[t], x_used[0])
            a = A(junk, h[:, t, :], ACT.Square, *h_ready[t], junk_used[0], accum=ss[:, t:t + 1])
            junk_used[0] = a
            rstd_ready[t] = rsqrt(rstd[:, t:t + 1], ss[:, t:t + 1], D, a, rstd_used[t])

        def in_chunk(evac, before=None, banks=(4, 5), lhs=None):
            us = take(2)
            lh, ll, ready = lhs or (xh, xl, x_ready)
            for t in range(2):
                if before:
                    before(t)
                b = banks[t]
                pe.wait(free[b])
                for j, u in enumerate(us):
                    pe.wait(lo_done[u], ready[t][j])
                    for k in range(4):
                        kk = 4 * j + k
                        tok = mm3(ps[b][:, :], lh[:, kk, P * t:P * t + P], ll[:, kk, P * t:P * t + P],
                                  whi[:, u % S, 512 * k:512 * k + 512], wlo[:, u % S, 512 * k:512 * k + 512],
                                  kk == 0, kk == 7, inc=k == 3)
                    if t == 1:
                        unit_done[u] = tok
                evac(t, b, tok)
            return tok

        def out_unit(k0, lh, ll, ready, first, last, each=None):
            u, = take(1)
            for t in range(2):
                pe.wait(lo_done[u], ready[t])
                if first:
                    pe.wait(free[2 * t], free[2 * t + 1])
                for k in range(2):
                    lhs = [x[:, k0 + k, P * t:P * t + P] for x in (lh, ll)]
                    for half in range(2):
                        c = 1024 * k + 512 * half
                        tok = mm3(ps[2 * t + half][:, :], lhs[0], lhs[1], whi[:, u % S, c:c + 512],
                                  wlo[:, u % S, c:c + 512], first and k == 0, last and k == 1,
                                  inc=k == 1 and half == 1)
                if each:
                    each(t, tok)
            unit_done[u] = tok
            return tok

        def residual(t, tok, weight=1.0):
            for half in range(2):
                cols = slice(512 * half, 512 * half + 512)
                b = 2 * t + half
                if weight == 1.0:
                    d = TT(h[:, t, cols], ps[b][:, :], h[:, t, cols], ALU.add, tok, h_ready[t][half])
                else:
                    d = STT(h[:, t, cols], ps[b][:, :], weight, h[:, t, cols], ALU.mult, ALU.add, tok,
                            h_ready[t][half])
                h_ready[t][half] = free[b] = d

        def square_out(lh, ll, ready, each):
            for n in range(4):
                tok = out_unit(2 * n, lh, ll, [ready[0][n // 2], ready[1][n // 2]], n == 0, n == 3,
                               each if n == 3 else None)
            return tok

        def ffn(name, weight):
            ht_ready = {}
            hid_read = [None, None]
            sil_read = [None, None]
            down_done = {}

            def evac(j):
                def f(t, b, tok):
                    a = A(sil[:, t, :], ps[b][:, 0:256], ACT.Silu, tok, rstd_ready[t], sil_read[t],
                          scale=rstd[:, t:t + 1])
                    d = STT(hid[:, t, :], ps[b][:, 256:512], rstd[:, t:t + 1], sil[:, t, :], ALU.mult, ALU.mult,
                            a, hid_read[t])
                    free[b] = sil_read[t] = rstd_used[t] = d
                    hid_done[t] = d
                return f

            def turn(j):
                b = tbank()
                for t in range(2):
                    for k in range(2):
                        tok = tr(ps[b][:, 256 * k + P * t:256 * k + P * t + P], hid[:, t, P * k:P * k + P],
                                 (hid_done[t], free[b]), inc=k == 1)
                    hid_read[t] = tok
                k0 = 2 * (j % 4)
                a = A(yh[:, k0:k0 + 2, :], ps[b][:, :].rearrange("p (k c) -> p k c", k=2), ACT.Copy, tok,
                      down_done.get(j - 4), y_used[0])
                d = TT(yl[:, k0:k0 + 2, :], ps[b][:, :].rearrange("p (k c) -> p k c", k=2),
                       yh[:, k0:k0 + 2, :].bitcast(F32), ALU.subtract, a)
                free[b] = ht_ready[j] = d

            hid_done = [None, None]
            for j in range(FC):
                x_tok = in_chunk(evac(j), before=(lambda t: norm(t, name)) if j == 0 else None)
                if j:
                    down_done[j - 1] = out_unit(2 * ((j - 1) % 4), yh, yl, [ht_ready[j - 1]] * 2, j == 1, False)
                turn(j)
            x_used[0] = x_tok
            down_done[FC - 1] = out_unit(2 * ((FC - 1) % 4), yh, yl, [ht_ready[FC - 1]] * 2, False, True,
                                         lambda t, tok: residual(t, tok, weight))
            y_used[0] = down_done[FC - 1]

        def ar(start, *shape):
            n = 1
            for s in shape:
                n *= s
            v = AR[:, start:start + n]
            names = "abcd"[:len(shape)]
            if len(shape) > 1:
                v = v.rearrange(f"p ({' '.join(names)}) -> p {' '.join(names)}",
                                **{c: s for c, s in zip(names, shape)})
            return v

        tok_x = [load(h[:, t, :], xin[t]) for t in range(2)]
        tok_k = load(kc[:, :], cst)
        tok_p = load(pr[:, :], par)
        pump()
        for t in range(2):
            h_ready[t] = [tok_x[t], tok_x[t]]
        pe.wait(tok_k)
        dve.wait(tok_p, tok_k)
        act.wait(tok_p, tok_k)
        pool.wait(tok_k)

        wgr = ar(0, 128)
        wg2s = AR[0:16, 128:384]
        bg = ar(384, 256)
        tok_wg = load(wgr, wg)
        tok_wg2 = load(wg2s, wg2)
        tok_bg = load(bg, brow["b_gate"])
        gqn = ar(640, 2, 512)
        gvn = ar(1664, 2, 512)
        srn = ar(2688, 2, 512)
        svn = ar(3712, 2, 512)
        sqn = ar(4736, 2, 512)
        sqT = ar(5760, 4, T)
        skT = ar(6784, 4, T)
        tmp = ar(7808, 2, 512)
        mixn = ar(8832, 2, D)
        gqT = ar(10880, 2, T)
        la = ar(11392, 2, T)
        zt = ar(11904, 3, 384)
        wgh = sb("wgh", [P, 128], F32R)
        wgl = sb("wgl", [P, 128], F32R)
        g_a = act.do(lambda e: e.copy(wgh[:, :], wgr), tok_wg)
        g_d = TT(wgl[:, :], wgr, wgh[:, :].bitcast(F32), ALU.subtract, g_a)
        gq8 = st[:, 4:5]
        gq8_t = TS(gq8, parm("gq"), 0.125, None, ALU.mult, None)

        read = {}

        def heads_evac(dst, gain, gain_tok, key):
            def f(t, b, tok):
                a = A(sqn[:, t, :], ps[b][:, :], ACT.Copy, tok, rstd_ready[t], read.get(("sqn", t)),
                      scale=rstd[:, t:t + 1])
                free[b] = a
                q3 = sqn[:, t, :].rearrange("p (h d) -> p h d", h=8)
                t3 = tmp[:, t, :].rearrange("p (h d) -> p h d", h=8)
                s8 = st[:, 8 + 8 * t:16 + 8 * t]
                d = TT(tmp[:, t, :], sqn[:, t, :], sqn[:, t, :], ALU.mult, a, read.get(("tmp", t)))
                d = dve.do(lambda e: e.tensor_reduce(s8, t3, AXX, ALU.add), d)
                d = rsqrt(s8, s8, 64, d)
                d = TT(t3, q3, s8.unsqueeze(2).to_broadcast([P, 8, 64]), ALU.mult, d)
                read[("sqn", t)] = d
                b2 = tbank()
                for i in range(4):
                    tk = tr(ps[b2][:, P * i:P * i + P], tmp[:, t, P * i:P * i + P], (d, free[b2]), inc=i == 3)
                read[("tmp", t)] = tk
                free[b2] = key[t] = A(dst[:, :, P * t:P * t + P], ps[b2][:, :].rearrange("p (k c) -> p k c", k=4),
                                      ACT.Copy, tk, gain_tok, scale=gain)
            return f

        def plain(dst, key, func=ACT.Copy):
            def f(t, b, tok):
                free[b] = key[t] = A(dst[:, t, :], ps[b][:, :], func, tok, rstd_ready[t], scale=rstd[:, t:t + 1])
            return f

        sq_t, sk_t, sv_t, gqk_t, gv_t, gr_t = ([None, None] for _ in range(6))
        in_chunk(heads_evac(sqT, gq8, gq8_t, sq_t), before=lambda t: norm(t, "mix0"))
        in_chunk(heads_evac(skT, parm("gk"), None, sk_t))
        in_chunk(plain(svn, sv_t))

        b = tbank()
        pe.wait(free[b], g_d)
        for t in range(2):
            for k in range(8):
                tok = mm3(ps[b][:, 16 * t:16 * t + 16], xh[:, k, P * t:P * t + P], xl[:, k, P * t:P * t + P],
                          wgh[:, 16 * k:16 * k + 16], wgl[:, 16 * k:16 * k + 16], k == 0, k == 7, inc=k == 7)
        glr = ar(13056, 2, 16)
        glT = AR[0:16, 13088:13344]
        for t in range(2):
            a = A(glr[:, t, :], ps[b][:, 16 * t:16 * t + 16], ACT.Copy, tok, junk_used[0], scale=rstd[:, t:t + 1])
        free[b] = a
        b = tbank()
        for t in range(2):
            tok = tr(ps[b][0:16, P * t:P * t + P], glr[:, t, :], (a, free[b]), inc=t == 1)
        a = A(glT, ps[b][0:16, 0:256], ACT.Copy, tok)
        free[b] = a
        b = tbank()
        pe.wait(a, tok_wg2, free[b])
        for t in range(2):
            tok = mm(ps[b][:, 256 * t:256 * t + 256], glT[:, P * t:P * t + P], wg2s, inc=t == 1)
        la2 = la.rearrange("p a b -> p (a b)")
        e1 = ar(7808, 512)
        d = dve.do(lambda e: e.tensor_tensor(la, ps[b][:, :].rearrange("p (a c) -> p a c", a=2),
                                             bg.unsqueeze(1).to_broadcast([P, 2, 256]), ALU.add), tok, tok_bg)
        free[b] = d
        a = A(e1, la2, ACT.Abs, d, *[read[("tmp", t)] for t in range(2)])
        a = A(e1, e1, ACT.Exp, a, scale=-1.0)
        a = A(e1, e1, ACT.Ln, a, bias=1.0)
        la_t = STT(la2, la2, 0.0, e1, ALU.min, ALU.subtract, a)
        read["tmp"] = la_t

        mask2 = const("mask", 256).rearrange("p (a c) -> p a c", a=2)
        zr = {}

        def z_head(i):
            pr0, j = 64 * (i % 2), i // 2
            kT, qT = skT[pr0:pr0 + 64, j, :], sqT[pr0:pr0 + 64, j, :]
            z, bt = ps[0], ps[1]
            pe.wait(free[0], *sq_t, *sk_t)
            mm(z[:, 0:256], kT[:, 0:128], qT[:, 0:256], inc=False)
            tok = mm(z[:, 256:384], kT[:, 128:256], qT[:, 128:256])
            ls, kp, sp_ = zt[:, 0, :], zt[:, 1, :], zt[:, 2, :]
            a = A(sp_, z[:, 0:384], ACT.Abs, tok, zr.get("sp"))
            a = A(sp_, sp_, ACT.Exp, a, scale=-1.0)
            a = A(sp_, sp_, ACT.Ln, a, bias=1.0)
            d = STT(ls, z[:, 0:384], 0.0, sp_, ALU.min, ALU.subtract, a, zr.get("ls"))
            d = TT(kp, ls, z[:, 0:384], ALU.subtract, d, zr.get("kp"))
            free[0] = d
            kd = kp.rearrange("p (a c) -> p a c", a=3)[:, 0:3:2, :]
            d = TT(kd, kd, mask2, ALU.mult, d)
            pe.wait(free[1], d)
            mm(bt[:, 0:256], const("later"), kp[:, 0:256], start=True, stop=False, skip=True, inc=False)
            mm(bt[:, 128:256], const("ones"), kp[:, 256:384], start=False, stop=False, skip=True, inc=False)
            tok = mm(bt[:, 256:384], const("later"), kp[:, 256:384], start=False, stop=True, skip=True)
            zr["kp"] = tok
            d = TT(sp_, ls, bt[:, 0:384], ALU.add, tok)
            free[1] = zr["ls"] = d
            a = A(sp_, sp_, ACT.Exp, d)
            wd = sp_.rearrange("p (a c) -> p a c", a=3)[:, 0:3:2, :]
            d = TT(wd, wd, mask2, ALU.mult, a)
            pe.wait(free[2], free[3], d, *sv_t)
            hc = slice(64 * i, 64 * i + 64)
            mm(ps[2][:, hc], sp_[:, 0:128], svn[:, 0, hc], inc=False)
            mm(ps[3][:, hc], sp_[:, 128:256], svn[:, 0, hc], start=True, stop=False, inc=False)
            zr["sp"] = mm(ps[3][:, hc], sp_[:, 256:384], svn[:, 1, hc], start=False, stop=True)

        z_head(0)
        z_head(1)
        in_chunk(plain(gqn, gqk_t))
        z_head(2)
        z_head(3)
        in_chunk(plain(gvn, gv_t))
        z_head(4)
        z_head(5)
        x_used[0] = in_chunk(plain(srn, gr_t, ACT.Silu))
        z_head(6)
        z_head(7)
        for t in range(2):
            free[2 + t] = A(mixn[:, t, 512:1024], ps[2 + t][:, :], ACT.Copy, zr["sp"])
        sb_done = [free[2], free[3]]

        b = tbank()
        for j in range(2):
            for t in range(2):
                c = 256 * j + P * t
                tok = tr(ps[b][:, c:c + P], gqn[:, t, P * j:P * j + P], (gqk_t[t], free[b]), inc=j == 1 and t == 1)
        a_q = A(gqT, ps[b][:, :].rearrange("p (j c) -> p j c", j=2), ACT.Copy, tok, scale=0.125)
        free[b] = a_q
        b = tbank()
        pe.wait(free[b], la_t)
        for t in range(2):
            tok = mm(ps[b][:, 256 * t:256 * t + 256], const("rest"), la[:, t, :], inc=t == 1)
        e_t = A(e1, ps[b][:, :], ACT.Exp, tok, la_t, scale=1.0 / 16)
        free[b] = e_t
        b = tbank()
        pe.wait(free[b])
        for j in range(2):
            for t in range(2):
                c = 4 * j + 2 * t
                tok = mm(ps[b][:, c:c + 2], la[:, t, P * j:P * j + P], const("blk", 2), inc=j == 1 and t == 1)
        dec = st[:, 24:32]
        dec_t = A(dec, ps[b][:, 0:8], ACT.Exp, tok, scale=1.0 / 16)
        free[b] = dec_t
        e3 = e1.rearrange("p (t c) -> p t c", t=2)
        ke_t = TT(gqn[:, :, 256:512], gqn[:, :, 256:512], e3, ALU.mult, e_t, *gqk_t)
        sts = [sb(f"state{n}", [P, 2, 256]) for n in range(2)]
        zer = [pool.do(lambda e, n=n: e.memset(sts[n][:, :, :], 0.0)) for n in range(2)]
        o_done = {}
        for n in range(4):
            t, c = divmod(n, 2)
            rows = slice(64 * c, 64 * c + 64)
            ub = n % 2
            pe.wait(free[ub], ke_t, *gv_t)
            for j in range(2):
                tok = mm(ps[ub][:, 256 * j:256 * j + 256], gqn[rows, t, 256 + P * j:256 + P * j + P],
                         gvn[rows, t, 256 * j:256 * j + 256], inc=j == 1)
            cur, prev = sts[n % 2], sts[(n + 1) % 2]
            for g in range(2):
                rr, cc = slice(64 * g, 64 * g + 64), slice(P * g, P * g + P)
                for j in range(2):
                    uu = ps[ub][rr, 256 * j + P * g:256 * j + P * g + P]
                    if n == 0:
                        d = dve.do(lambda e, o=cur[rr, j, cc], i=uu: e.tensor_copy(o, i), tok, *zer)
                    else:
                        d = STT(cur[rr, j, cc], prev[rr, j, cc], st[rr, 24 + 4 * j + n:25 + 4 * j + n], uu,
                                ALU.mult, ALU.add, tok, dec_t, o_done.get(n - 2), s_done)
            s_done = free[ub] = d
            pe.wait(d, a_q, free[2 + t])
            for j in range(2):
                o_done[n] = mm(ps[2 + t][rows, 256 * j:256 * j + 256], gqT[:, j, 64 * n:64 * n + 64],
                               cur[:, j, :], inc=j == 1)
        y_ready = [None, None]
        for t in range(2):
            m = mixn[:, t, 0:512]
            m3 = m.rearrange("p (h d) -> p h d", h=4)
            tp = sqn[:, t, :]
            tp3 = tp.rearrange("p (h d) -> p h d", h=4)
            a = A(m, ps[2 + t][:, :], ACT.Copy, o_done[2 * t + 1])
            free[2 + t] = a
            s4 = st[:, 32 + 4 * t:36 + 4 * t]
            d = TT(tp, m, m, ALU.mult, a)
            d = dve.do(lambda e, s4=s4, tp3=tp3: e.tensor_reduce(s4, tp3, AXX, ALU.add), d)
            d = rsqrt(s4, s4, 128, d)
            d = TT(m3, m3, s4.unsqueeze(2).to_broadcast([P, 4, 128]), ALU.mult, d)
            d = TT(m, m, srn[:, t, :], ALU.mult, d, gr_t[t])
            y_ready[t] = xpose(mixn[:, t, :], t, yh, yl, lambda k: parm("gla") if k < 4 else None,
                               [d, sb_done[t]], y_used[0])
        y_used[0] = square_out(yh, yl, y_ready, residual)

        arena_free = [y_used[0], list(free)]
        ffn("ffn0", 1.0)

        bp1 = ar(0, 2048)
        bp2 = ar(2048, 1024)
        t_bp1 = load(bp1, brow["b_pw1"], *arena_free)
        t_bp2 = load(bp2, brow["b_pw2"])
        glu = ar(3072, 2, 512)
        upad = ar(4096, 8, 286)
        cv = ar(6384, 8, T)
        sq = ar(8432, 8, T)
        mu = ar(10480, 2, T)
        u2 = ar(10992, 2, 512)
        z0 = pool.do(lambda e: e.memset(upad[:, :, 0:30], 0.0), *arena_free)
        gl_read = {}
        cvt = [None] * 8
        hb = []

        def glu_evac(j):
            def f(t, b, tok):
                ga, gb = glu[:, t, 0:256], glu[:, t, 256:512]
                bias = bp1[:, 512 * j:512 * j + 512]
                d = STT(glu[:, t, :], ps[b][:, :], rstd[:, t:t + 1], bias, ALU.mult, ALU.add, tok, t_bp1,
                        rstd_ready[t], gl_read.get(t))
                free[b] = rstd_used[t] = d
                a = A(gb, gb, ACT.Sigmoid, d)
                d = TT(u2[:, t, 0:256], ga, gb, ALU.mult, a, gl_read.get(t))
                gl_done[t] = d
            return f

        gl_done = [None, None]
        for j in range(4):
            tokc = in_chunk(glu_evac(j), before=(lambda t: norm(t, "mix1")) if j == 0 else None)
            b = tbank()
            for t in range(2):
                for k in range(2):
                    tok = tr(ps[b][:, 256 * k + P * t:256 * k + P * t + P], u2[:, t, P * k:P * k + P],
                             (gl_done[t], free[b]), inc=k == 1)
                gl_read[t] = tok
            a = A(upad[:, 2 * j:2 * j + 2, 30:286], ps[b][:, :].rearrange("p (k c) -> p k c", k=2), ACT.Copy, tok, z0)
            free[b] = a
            for c in (2 * j, 2 * j + 1):
                d = TS(cv[:, c, :], upad[:, c, 0:256], parm("w_dw", 31 * c), parm("b_dw", c), ALU.mult, ALU.add, a,
                       z0)
                for w in range(1, 31):
                    d = STT(cv[:, c, :], upad[:, c, w:w + 256], parm("w_dw", 31 * c + w), cv[:, c, :], ALU.mult,
                            ALU.add, d)
                cvt[c] = d
        x_used[0] = tokc
        pe.wait(free[0])
        for c in range(8):
            tok = mm(ps[0][:, 0:256], const("ones"), cv[:, c, :], start=c == 0, stop=c == 7, deps=(cvt[c],),
                     inc=c == 7)
        a = A(mu[:, 0, :], ps[0][:, 0:256], ACT.Copy, tok, scale=1.0 / D)
        free[0] = a
        d = TT(cv, cv, mu[:, 0:1, :].to_broadcast([P, 8, T]), ALU.subtract, a)
        a = A(sq, cv, ACT.Square, d)
        pe.wait(free[1])
        for c in range(8):
            tok = mm(ps[1][:, 0:256], const("ones"), sq[:, c, :], start=c == 0, stop=c == 7, deps=(a,), inc=c == 7)
        d2 = rsqrt(mu[:, 1, :], ps[1][:, 0:256], D, tok)
        free[1] = d2
        d = TT(cv, cv, mu[:, 1:2, :].to_broadcast([P, 8, T]), ALU.mult, d2, a)
        for t in range(2):
            for half in range(2):
                cols = slice(512 * half, 512 * half + 512)
                h_ready[t][half] = TT(h[:, t, cols], h[:, t, cols], bp2[:, cols], ALU.add, h_ready[t][half], t_bp2,
                                      x_ready[t], junk_used[0])
        done = []
        for half in range(2):
            for c in range(4 * half, 4 * half + 4):
                a = A(cv[:, c, :], cv[:, c, :], ACT.Silu, d, scale=parm("ln_g", c), bias=parm("ln_b", c))
            cs = slice(4 * half, 4 * half + 4)
            a = A(yh[:, cs, :], cv[:, cs, :], ACT.Copy, a, y_used[0])
            done.append(TT(yl[:, cs, :], cv[:, cs, :], yh[:, cs, :].bitcast(F32), ALU.subtract, a))
        y_used[0] = square_out(yh, yl, [done, done], residual)

        arena_free = [y_used[0], list(free)]
        ffn("ffn1", 1.0)
        ffn("n1", 0.5)

        gb = ar(0, 2048)
        cosn = ar(2048, 2, 2, 128)
        rm = ar(2560, 4, 384)
        pm = ar(4096, 4, 384)
        t_gb = load(gb, brow["gate_bias"], *arena_free)
        t_cs = load(cosn.rearrange("p a b c -> p (a b c)"), cosin)
        t_rm = load(rm.rearrange("p a b -> p (a b)"), rmask)
        t_pm = load(pm.rearrange("p a b -> p (a b)"), pmat)
        merged = ar(5632, 2, D)
        qT = ar(7680, 4, T)
        kT = ar(8704, 4, T)
        vn = ar(9728, 2, 1024)
        pn = ar(9728, 2, 1024)
        ro = ar(11776, 2, 512)
        sc = ar(12800, 384)
        gt = ar(13184, 512)
        sc_read, gt_read, ro_read = [None], [None], [None, None]

        p_t = [[None, None], [None, None]]

        def p_evac(j):
            def f(t, b, tok):
                free[b] = p_t[j][t] = A(pn[:, t, 512 * j:512 * j + 512], ps[b][:, :], ACT.Copy, tok, rstd_ready[t],
                                        scale=rstd[:, t:t + 1])
            return f

        for j in range(2):
            in_chunk(p_evac(j), before=(lambda t: norm(t, "nm")) if j == 0 else None)
        pl_ready = []
        for c in range(8):
            g = c // 2
            if c % 2 == 0:
                b = tbank()
                pe.wait(free[b], *p_t[c // 4], t_pm)
            o = 256 * (c % 2)
            cols = slice(P * c, P * c + P)
            mm(ps[b][:, o:o + 256], pn[:, 0, cols], pm[:, g, 0:256], start=c % 2 == 0, stop=False, skip=True,
               inc=False)
            tok = mm(ps[b][:, o + 128:o + 256], pn[:, 1, cols], pm[:, g, 256:384], start=False, stop=True, skip=True)
            if c % 2:
                a = A(yh[:, c - 1:c + 1, :], ps[b][:, :].rearrange("p (k c) -> p k c", k=2), ACT.Copy, tok, y_used[0])
                d = TT(yl[:, c - 1:c + 1, :], ps[b][:, :].rearrange("p (k c) -> p k c", k=2),
                       yh[:, c - 1:c + 1, :].bitcast(F32), ALU.subtract, a)
                free[b] = d
                pl_ready.append(d)
        pn_read = tok
        u, = take(1)
        pe.wait(lo_done[u])
        for g in range(4):
            pe.wait(free[g], pl_ready[g])
            for dd in range(2):
                for cc in range(2):
                    c = 512 * g + 256 * cc + P * dd
                    tok = mm3(ps[g][:, 256 * dd:256 * dd + 256], whi[:, u % S, c:c + P], wlo[:, u % S, c:c + P],
                              yh[:, 2 * g + cc, :], yl[:, 2 * g + cc, :], cc == 0, cc == 1, inc=cc == 1)
            free[g] = tok
        unit_done[u] = tok
        pool_ready = []
        for g in range(4):
            for dd in range(2):
                k = 2 * g + dd
                a = A(yh[:, k, :], ps[g][:, 256 * dd:256 * dd + 256], ACT.Copy, tok, scale=parm("pool", k))
            for dd in range(2):
                k = 2 * g + dd
                d = STT(yl[:, k, :], ps[g][:, 256 * dd:256 * dd + 256], parm("pool", k), yh[:, k, :].bitcast(F32),
                        ALU.mult, ALU.subtract, a)
            free[g] = d
            pool_ready.append(d)
        pool_r = [[pool_ready[1], pool_ready[3]]] * 2
        gate_t = {}

        def gate_evac(which, j):
            def f(t, b, tok):
                g_ = sigt[:, t, :]
                d = STT(g_, ps[b][:, :], rstd[:, t:t + 1], gb[:, 1024 * which + 512 * j:1024 * which + 512 * j + 512],
                        ALU.mult, ALU.add, tok, rstd_ready[t], t_gb, gate_t.get(("read", t)))
                free[b] = rstd_used[t] = d
                gate_t[t] = A(g_, g_, ACT.Sigmoid, d)
            return f

        mg_t = {}

        def up_evac(which, j):
            def f(t, b, tok):
                g_ = sigt[:, t, :]
                m = merged[:, t, 512 * j:512 * j + 512]
                if which == 1:
                    d = TT(m, ps[b][:, :], g_, ALU.mult, tok, gate_t[t])
                else:
                    d = TT(g_, ps[b][:, :], g_, ALU.mult, tok, gate_t[t])
                free[b] = d
                if which == 0:
                    d = TT(m, m, g_, ALU.add, d, mg_t[(j, t)])
                mg_t[(j, t)] = d
                gate_t[("read", t)] = d
            return f

        sigt = ar(11776, 2, 512)
        for j in range(2):
            in_chunk(gate_evac(1, j))
            tok_y = in_chunk(up_evac(1, j), banks=(0, 1), lhs=(yh, yl, pool_r))
        y_used[0] = tok_y
        ro_read = [gate_t[("read", 0)], gate_t[("read", 1)]]

        def rot_evac(dst, ready, j):
            def f(t, b, tok):
                x = ps[b][:, :].rearrange("p (h a d) -> p h a d", h=2, a=2)
                o = ro[:, t, :].rearrange("p (h a d) -> p h a d", h=2, a=2)
                w = rtmp[:, :].rearrange("p (h d) -> p h d", h=2)
                cs_, sn = (cosn[:, t, i:i + 1, :].to_broadcast([P, 2, 128]) for i in range(2))
                r_ = rstd[:, t:t + 1]
                d1 = STT(o[:, :, 0, :], x[:, :, 0, :], r_, cs_, ALU.mult, ALU.mult, tok, rstd_ready[t], t_cs,
                         ro_read[t])
                d2 = STT(w, x[:, :, 1, :], r_, sn, ALU.mult, ALU.mult, rt_read[0])
                d1 = TT(o[:, :, 0, :], o[:, :, 0, :], w, ALU.subtract, d1, d2)
                d2 = STT(w, x[:, :, 0, :], r_, sn, ALU.mult, ALU.mult, d1)
                d3 = STT(o[:, :, 1, :], x[:, :, 1, :], r_, cs_, ALU.mult, ALU.mult)
                free[b] = d3
                d = TT(o[:, :, 1, :], o[:, :, 1, :], w, ALU.add, d3)
                rt_read[0] = d
                b2 = tbank()
                for i in range(4):
                    tk = tr(ps[b2][:, P * i:P * i + P], ro[:, t, P * i:P * i + P], (d, free[b2]), inc=i == 3)
                ro_read[t] = tk
                free[b2] = ready[t] = A(dst[:, :, P * t:P * t + P],
                                        ps[b2][:, :].rearrange("p (k c) -> p k c", k=4), ACT.Copy, tk,
                                        tr_read.get(id(dst)))
            return f

        rtmp = ar(13184, 256)
        rt_read = [None]
        tr_read = {}
        v_t = [[None, None], [None, None]]

        def v_evac(j):
            def f(t, b, tok):
                free[b] = v_t[j][t] = A(vn[:, t, 512 * j:512 * j + 512], ps[b][:, :], ACT.Copy, tok, rstd_ready[t],
                                        pn_read, scale=rstd[:, t:t + 1])
            return f

        def ret_head(i, q_r, k_r):
            hh = 2 * (i % 2)
            pe.wait(free[0], *q_r, *k_r)
            for c in range(2):
                mm(ps[0][:, 0:256], kT[:, hh + c, 0:128], qT[:, hh + c, :], start=c == 0, stop=c == 1, inc=False)
            for c in range(2):
                tok = mm(ps[0][:, 256:384], kT[:, hh + c, 128:256], qT[:, hh + c, 128:256], start=c == 0,
                         stop=c == 1, inc=c == 1)
            d = TT(sc, ps[0][:, 0:384], rm[:, i, :], ALU.mult, tok, t_rm, sc_read[0])
            free[0] = d
            vc = slice(256 * i, 256 * i + 256)
            pe.wait(d, free[2], free[3], *v_t[i // 2])
            c0 = 256 * (i % 2)
            a0 = mm(ps[2][:, c0:c0 + 256], sc[:, 0:128], vn[:, 0, vc])
            mm(ps[3][:, c0:c0 + 256], sc[:, 128:256], vn[:, 0, vc], start=True, stop=False, inc=False)
            sc_read[0] = mm(ps[3][:, c0:c0 + 256], sc[:, 256:384], vn[:, 1, vc], start=False, stop=True)
            return sc_read[0]

        retn = {}
        ret_t = {}

        def gret_evac(j):
            def f(t, b, tok):
                a = A(gt, ps[b][:, :], ACT.Silu, tok, rstd_ready[t], gt_read[0], rt_read[0], scale=rstd[:, t:t + 1])
                free[b] = a
                v_ = vn[:, t, 512 * j:512 * j + 512]
                d = TT(v_, v_, gt, ALU.mult, a, ret_t[(j, t)])
                gt_read[0] = ret_t[(j, t)] = d
            return f

        for j in range(2):
            in_chunk(v_evac(j))
        for j in range(2):
            q_r, k_r = [None, None], [None, None]
            in_chunk(rot_evac(qT, q_r, j))
            in_chunk(rot_evac(kT, k_r, j))
            for i in (2 * j, 2 * j + 1):
                last = ret_head(i, q_r, k_r)
            tr_read[id(qT)] = tr_read[id(kT)] = last
            for t in range(2):
                v_ = vn[:, t, 512 * j:512 * j + 512]
                v3 = v_.rearrange("p (h d) -> p h d", h=2)
                a = A(v_, ps[2 + t][:, :], ACT.Copy, last)
                free[2 + t] = a
                s2 = st[:, 40 + 4 * j + 2 * t:42 + 4 * j + 2 * t]
                r3 = ro[:, t, :].rearrange("p (h d) -> p h d", h=2)
                d = TT(ro[:, t, :], v_, v_, ALU.mult, a, ro_read[t])
                d = dve.do(lambda e, s2=s2, r3=r3: e.tensor_reduce(s2, r3, AXX, ALU.add), d)
                ro_read[t] = d
                d = rsqrt(s2, s2, 256, d)
                ret_t[(j, t)] = TT(v3, v3, s2.unsqueeze(2).to_broadcast([P, 2, 256]), ALU.mult, d)
        for j in range(2):
            in_chunk(gret_evac(j))
        for t in range(2):
            y_ready[t] = xpose(vn[:, t, :], t, yh, yl, lambda k: None, [ret_t[(0, t)], ret_t[(1, t)]], y_used[0])
        gate_t.clear()
        for t in range(2):
            gate_t[("read", t)] = ro_read[t]
        for j in range(2):
            x_used[0] = in_chunk(gate_evac(0, j))
            tok_y = in_chunk(up_evac(0, j), banks=(0, 1), lhs=(yh, yl, y_ready))
        y_used[0] = tok_y
        for t in range(2):
            y_ready[t] = xpose(merged[:, t, :], t, yh, yl, lambda k: None, [mg_t[(0, t)], mg_t[(1, t)]], y_used[0])
        y_used[0] = square_out(yh, yl, y_ready, residual)
        arena_free = [y_used[0], list(free)]
        ffn("n2", 0.5)

        fin = ar(0, 1024)
        t_f = load(fin, brow["norm_final"], *arena_free)
        res = ar(1024, 2, D)
        stores = []
        for t in range(2):
            a = A(junk, h[:, t, :], ACT.Square, *h_ready[t], junk_used[0], accum=ss[:, t:t + 1])
            junk_used[0] = a
            d = rsqrt(rstd[:, t:t + 1], ss[:, t:t + 1], D, a, rstd_used[t])
            d = STT(res[:, t, :], h[:, t, :], rstd[:, t:t + 1], fin, ALU.mult, ALU.mult, d, t_f, arena_free)
            sem = ctx.enter_context(nc.semaphore(f"stored{t}"))
            sp.wait(d)
            sp.items.append(lambda e, t=t, sem=sem: e.dma_start(out[t], res[:, t, :]).then_inc(sem, 16))
            stores.append((sem, 16))
        sp.wait(*stores)
        assert at[0] == NU

        block = ctx.enter_context(nc.Block())

        @block.sync
        def _(e):
            for f in sp.items:
                f(e)

        @block.tensor
        def _(e):
            for f in pe.items:
                f(e)

        @block.scalar
        def _(e):
            for f in act.items:
                f(e)

        @block.vector
        def _(e):
            for f in dve.items:
                f(e)

        @block.gpsimd
        def _(e):
            for f in pool.items:
                f(e)


def constants():
    import numpy as np
    i = np.arange(128)
    cst = np.zeros((128, NKW), np.float32)
    cst[:, 0:128] = np.eye(128)
    cst[:, 128:256] = i[:, None] > i[None, :]
    cst[:, 256:384] = 1
    cst[:, 384:512] = cst[:, 512:640] = i[:, None] < i[None, :]
    cst[:, 640:768] = (i[:, None] > i[None, :]) & (i[:, None] // 64 == i[None, :] // 64)
    cst[:, 768:770] = i[:, None] // 64 == np.arange(2)[None, :]
    half = 128
    inv = (np.float32(10000.0) ** (-np.arange(half, dtype=np.float32) / np.float32(half))).astype(np.float32)
    ang = np.arange(256, dtype=np.float32)[:, None] * inv[None, :]
    cs = np.stack([np.cos(ang), np.sin(ang)], axis=1).astype(np.float32)
    cosin = np.ascontiguousarray(cs.reshape(2, 128, 2, 128).transpose(1, 0, 2, 3).reshape(128, 512))
    s = np.arange(256)
    rmask = np.zeros((128, 4, 384), np.float32)
    for g in range(4):
        gamma = 1.0 - 2.0 ** (-5.0 - g)
        m = np.where(s[:, None] // 64 <= s[None, :] // 64, gamma ** np.abs(s[:, None] - s[None, :]), 0.0) / 16.0
        rmask[:, g, 0:256] = m[0:128]
        rmask[:, g, 256:384] = m[128:256, 128:256]
    pmat = np.zeros((128, 4, 384), np.float32)
    for g, w in enumerate((2, 4, 8, 16)):
        d = s[None, :] - s[:, None]
        m = ((d >= 0) & (d < w)) / np.minimum(s[None, :] + 1.0, w) - (d == 0)
        pmat[:, g, 0:256] = m[0:128]
        pmat[:, g, 256:384] = m[128:256, 128:256]
    return cst, cosin, rmask.reshape(128, -1), pmat.reshape(128, -1)


def units_in(w):
    n = w.shape[1] // 512
    return w.reshape(2, 4, 128, n, 512).transpose(3, 0, 2, 1, 4).reshape(2 * n, 128, 2048)


def units_out(w):
    n = w.shape[0] // 256
    return w.reshape(n, 2, 128, 1024).transpose(0, 2, 1, 3).reshape(n, 128, 2048)


def units_ffn(wg, wu, wd):
    import numpy as np
    pair = np.stack([wg.reshape(1024, FC, 256), wu.reshape(1024, FC, 256)], axis=2).reshape(1024, FC * 512)
    a, b = units_in(pair), units_out(wd)
    seq = [a[0], a[1]]
    for j in range(1, FC):
        seq += [a[2 * j], a[2 * j + 1], b[j - 1]]
    seq.append(b[FC - 1])
    return seq


def layout(i):
    import numpy as np
    cst, cosin, rmask, pmat = constants()
    win = i["hy_w_in"][0]
    col = {}
    c = 0
    for n, w in (("gq", 256), ("gk", 256), ("gv", 512), ("gr", 512), ("glr", 16), ("sq", 512), ("sk", 512),
                 ("sv", 512)):
        col[n] = win[:, c:c + w]
        c += w
    seq = []
    for n in ("sq", "sk", "sv"):
        seq += list(units_in(col[n]))
    seq += list(units_in(np.concatenate([col["gq"], col["gk"]], axis=1)))
    seq += list(units_in(col["gv"])) + list(units_in(col["gr"]))
    seq += list(units_out(i["hy_w_out"][0]))
    seq += units_ffn(i["ffn_w_gate"][0], i["ffn_w_up"][0], i["ffn_w_down"][0])
    pw = i["cv_w_pw1"][0].reshape(1024, 2, 4, 256).transpose(0, 2, 1, 3).reshape(1024, 2048)
    seq += list(units_in(pw)) + list(units_out(i["cv_w_pw2"][0]))
    seq += units_ffn(i["ffn_w_gate"][1], i["ffn_w_up"][1], i["ffn_w_down"][1])
    f1 = i["ffn1_w_in_2"][0]
    seq += units_ffn(f1[:, :2816], f1[:, 2816:], i["ffn1_w_out_2"][0])
    w2 = i["w_in_2"][0]
    q, k, v, g, p = (w2[:, 1024 * n:1024 * n + 1024] for n in range(5))
    g0, g1 = w2[:, 5120:6144], w2[:, 6144:7168]
    seq += list(units_in(p))
    seq.append(i["pool_w_2"][0].reshape(4, 2, 128, 256).transpose(2, 0, 1, 3).reshape(128, 2048))
    a, b = units_in(g1), units_in(i["w_pool_up_2"][0])
    seq += [*a[0:2], *b[0:2], *a[2:4], *b[2:4]]
    seq += list(units_in(v))
    a, b = units_in(q), units_in(k)
    seq += [*a[0:2], *b[0:2], *a[2:4], *b[2:4]]
    seq += list(units_in(g))
    a, b = units_in(g0), units_in(i["w_ret_up_2"][0])
    seq += [*a[0:2], *b[0:2], *a[2:4], *b[2:4]]
    seq += list(units_out(i["w_out_2"][0]))
    f2 = i["ffn2_w_in_2"][0]
    seq += units_ffn(f2[:, :2816], f2[:, 2816:], i["ffn2_w_out_2"][0])

    def cols(x):
        return x.reshape(-1, 128).T

    def twice(x):
        return np.concatenate([x, x]).reshape(128, 1)

    par = np.concatenate([
        cols(i["mix_norm"][0]), cols(i["ffn_norm"][0]), cols(i["mix_norm"][1]), cols(i["ffn_norm"][1]),
        cols(i["norm_ffn1_2"][0]), cols(i["norm_mix_2"][0]), cols(i["norm_ffn2_2"][0]), cols(i["hy_gla_norm"][0]),
        twice(i["hy_sb_q_norm"][0]), twice(i["hy_sb_k_norm"][0]), cols(i["cv_b_dw"][0]), cols(i["cv_ln_g"][0]),
        cols(i["cv_ln_b"][0]), cols(i["pool_scale_2"][0]),
        i["cv_w_dw"][0].reshape(31, 8, 128).transpose(2, 1, 0).reshape(128, 248)], axis=1)

    def rows(x):
        return np.broadcast_to(x.reshape(1, -1), (128, x.size))

    return {
        "x": i["x"].reshape(2, 128, 1024), "w": np.stack(seq),
        "wg": col["glr"].reshape(8, 128, 16).transpose(1, 0, 2).reshape(128, 128), "wg2": i["hy_w_gate2"][0],
        "cst": cst, "par": par, "b_gate": rows(i["hy_b_gate"][0]),
        "b_pw1": rows(i["cv_b_pw1"][0].reshape(2, 4, 256).transpose(1, 0, 2)),
        "b_pw2": rows(i["cv_b_pw2"][0]), "gate_bias": rows(i["gate_bias_2"][0]),
        "norm_final": rows(i["norm_final_2"]), "cosin": cosin, "rmask": rmask, "pmat": pmat,
    }


def kernel(**inputs):
    import numpy as np
    import concourse.bacc as bacc
    from concourse.bass_utils import run_bass_kernel_spmd
    laid = layout({k: np.asarray(v) for k, v in inputs.items()})
    nc = bacc.Bacc("TRN2", target_bir_lowering=False, num_devices=1)
    arrays, aps = {}, {}
    for name, a in laid.items():
        a = np.ascontiguousarray(a)
        arrays["in_" + name] = a
        aps[name] = nc.dram_tensor("in_" + name, a.shape, mybir.dt.from_np(a.dtype), kind="ExternalInput").ap()
    out = nc.dram_tensor("out_0", (2, 128, 1024), F32, kind="ExternalOutput").ap()
    build(nc, aps["x"], aps["w"], aps["wg"], aps["wg2"], aps["cst"], aps["par"],
          {n: aps[n] for n in ("b_gate", "b_pw1", "b_pw2", "gate_bias", "norm_final")}, aps["cosin"], aps["rmask"],
          aps["pmat"], out)
    r = run_bass_kernel_spmd(nc, [arrays], core_ids=[0])
    return r.results[0]["out_0"].reshape(1, 256, 1024)
```

```python
from contextlib import ExitStack

import concourse.bass as bass
from concourse import mybir

P = 128
D = 1024
T = 256
FC = 11
UC = 2048
R = 4
S = 4

F32 = mybir.dt.float32
F32R = mybir.dt.float32r
ALU = mybir.AluOpType
ACT = mybir.ActivationFunctionType
AXX = mybir.AxisListType.X

EPS = 1e-6
NK = {"ident": 0, "later": 128, "ones": 256, "mask": 384, "rest": 640, "blk": 768}
NKW = 770
PAR = {"mix0": 0, "ffn0": 8, "mix1": 16, "ffn1": 24, "n1": 32, "nm": 40, "n2": 48, "gla": 56, "gq": 57, "gk": 58,
       "b_dw": 59, "ln_g": 67, "ln_b": 75, "pool": 83, "w_dw": 91}
PARW = 91 + 8 * 31
UNITS = {"sq": 2, "sk": 2, "sv": 2, "gqk": 2, "gv": 2, "gr": 2, "hout": 4, "ff0": 33, "pw1": 8, "pw2": 4, "ff1": 33,
         "ffa": 33, "p": 4, "pw": 1, "gp": 8, "q": 4, "k": 4, "v": 4, "gret": 4, "gu": 8, "out2": 4, "ffb": 33}


def build(nc, xin, wst, wg, wg2, cst, par, brow, cosin, rmask, pmat, out):
    NU = wst.shape[0]
    assert NU == sum(UNITS.values())
    with ExitStack() as ctx:
        def sb(name, shape, dt=F32):
            return ctx.enter_context(nc.sbuf_tensor(name, shape, dt))

        class Engine:

            def __init__(self, name):
                self.name, self.items, self.count, self.seen = name, [], 0, {}
                self.sem = ctx.enter_context(nc.semaphore("done_" + name))

            def wait(self, *tokens):
                for tok in tokens:
                    if tok is None:
                        continue
                    if isinstance(tok, list):
                        self.wait(*tok)
                        continue
                    sem, value = tok
                    if self.seen.get(sem.name, 0) < value:
                        self.seen[sem.name] = value
                        self.items.append(lambda e, sem=sem, value=value: e.wait_ge(sem, value))

            def do(self, fn, *tokens, inc=True):
                self.wait(*tokens)
                if not inc:
                    self.items.append(fn)
                    return None
                self.count += 1
                self.items.append(lambda e: fn(e).then_inc(self.sem, 1))
                return self.sem, self.count

        pe, act, dve, pool, sp = Engine("pe"), Engine("act"), Engine("dve"), Engine("pool"), Engine("sp")

        raw = sb("raw", [P, R, UC])
        whi = sb("whi", [P, S, UC], F32R)
        wlo = sb("wlo", [P, S, UC], F32R)
        xh = sb("xh", [P, 8, T], F32R)
        xl = sb("xl", [P, 8, T], F32R)
        yh = sb("yh", [P, 8, T], F32R)
        yl = sb("yl", [P, 8, T], F32R)
        h = sb("h", [P, 2, D])
        kc = sb("kc", [P, NKW])
        pr = sb("pr", [P, PARW])
        st = sb("st", [P, 96])
        sil = sb("sil", [P, 2, T])
        hid = sb("hid", [P, 2, T])
        AR = sb("AR", [P, 14080])
        ps = [ctx.enter_context(nc.psum_tensor(f"ps{i}", [P, 512], F32)) for i in range(8)]
        free = [None] * 8

        def const(name, n=P):
            return kc[:, NK[name]:NK[name] + n]

        def parm(name, k=0, n=1):
            return pr[:, PAR[name] + k:PAR[name] + k + n]

        ident = const("ident")

        slot_sem = [ctx.enter_context(nc.semaphore(f"raw{i}")) for i in range(R)]

        def load(dst, src, *tokens):
            sem = ctx.enter_context(nc.semaphore(f"load{len(sp.items)}"))
            sp.wait(*tokens)
            sp.items.append(lambda e: e.dma_start(dst, src).then_inc(sem, 16))
            return sem, 16

        hi_done, lo_done, unit_done = {}, {}, {}
        loaded = [0]
        split = [0]

        def load_unit():
            v = loaded[0]
            if v < NU and (v < R or v - R in lo_done):
                sp.wait(lo_done.get(v - R))
                sem = slot_sem[v % R]
                sp.items.append(lambda e: e.dma_start(raw[:, v % R, :], wst[v]).then_inc(sem, 16))
                loaded[0] += 1
                return True
            return False

        def pump():
            while True:
                while load_unit():
                    pass
                v = split[0]
                if v >= NU or v >= loaded[0] or not (v < S or v - S in unit_done):
                    return
                split[0] += 1
                arrived = (slot_sem[v % R], 16 * (v // R + 1))
                hi_done[v] = act.do(lambda e, v=v: e.copy(whi[:, v % S, :], raw[:, v % R, :]),
                                    arrived, unit_done.get(v - S))
                lo_done[v] = dve.do(lambda e, v=v: e.tensor_tensor(wlo[:, v % S, :], raw[:, v % R, :],
                                                                   whi[:, v % S, :].bitcast(F32), ALU.subtract),
                                    hi_done[v], unit_done.get(v - S))

        at = [0]
        plan, here = {}, [0]

        def later(n, fn):
            plan.setdefault(here[0] + n, []).append(fn)

        def gap():
            for fn in plan.pop(here[0], []):
                fn()
            here[0] += 1

        def gaps_left():
            while plan:
                gap()

        def take(n):
            pump()
            us = list(range(at[0], at[0] + n))
            at[0] += n
            for u in us:
                assert u in lo_done
            return us

        def mm3(o, ah, al, bh, bl, start, stop, skip=False, inc=False):
            pe.do(lambda e: e.matmul(o, ah, bh, start=start, stop=False, skip_group_check=skip), inc=False)
            pe.do(lambda e: e.matmul(o, ah, bl, start=False, stop=False, skip_group_check=skip), inc=False)
            return pe.do(lambda e: e.matmul(o, al, bh, start=False, stop=stop, skip_group_check=skip), inc=inc)

        def mm(o, a, b, start=True, stop=True, skip=False, inc=True, deps=()):
            return pe.do(lambda e: e.matmul(o, a, b, start=start, stop=stop, skip_group_check=skip), *deps, inc=inc)

        def tr(o, i, deps=(), inc=True):
            return pe.do(lambda e: e.transpose(o, i, ident[0:i.shape[0], 0:i.shape[0]]), *deps, inc=inc)

        def A(out_, in_, func, *deps, scale=1.0, bias=0.0, accum=None):
            return act.do(lambda e: e.activation(out_, in_, func, bias=bias, scale=scale, accum_out=accum)
                          if accum is not None else e.activation(out_, in_, func, bias=bias, scale=scale), *deps)

        def TT(out_, a, b, op, *deps, eng=dve):
            return eng.do(lambda e: e.tensor_tensor(out_, a, b, op), *deps)

        def TS(out_, a, s1, s2, op0, op1, *deps, eng=dve):
            if op1 is None:
                return eng.do(lambda e: e.tensor_scalar(out_, a, s1, None, op0), *deps)
            return eng.do(lambda e: e.tensor_scalar(out_, a, s1, s2, op0, op1), *deps)

        def STT(out_, a, s, b, op0, op1, *deps):
            return dve.do(lambda e: e.scalar_tensor_tensor(out=out_, in0=a, scalar=s, in1=b, op0=op0, op1=op1), *deps)

        def rsqrt(out_, ss, n, *deps):
            a = TS(out_, ss, 1.0 / n, EPS, ALU.mult, ALU.add, *deps)
            return TT(out_, out_, nhalf[:, 0:out_.shape[1]], ALU.pow, a, nhalf_t, eng=pool)

        flip = [0]

        def tbank():
            flip[0] ^= 1
            return 6 + flip[0]

        def xpose_half(src, t, half, dh, dl, gain, ready, *freed):
            b = tbank()
            cols = slice(P * t, P * t + P)
            ks = range(4 * half, 4 * half + 4)
            for i, k in enumerate(ks):
                tok = tr(ps[b][:, 128 * i:128 * i + 128], src[:, 128 * k:128 * k + 128], (ready, free[b]), inc=i == 3)
            if all(gain(k) is None for k in ks):
                src4 = ps[b][:, :].rearrange("p (k c) -> p k c", k=4)
                hi4, lo4 = (x[:, 4 * half:4 * half + 4, cols] for x in (dh, dl))
                a = A(hi4, src4, ACT.Copy, tok, *freed)
                d = TT(lo4, src4, hi4.bitcast(F32), ALU.subtract, a)
            else:
                for i, k in enumerate(ks):
                    a = A(dh[:, k, cols], ps[b][:, 128 * i:128 * i + 128], ACT.Copy, tok, *freed, scale=gain(k))
                for i, k in enumerate(ks):
                    d = STT(dl[:, k, cols], ps[b][:, 128 * i:128 * i + 128], gain(k),
                            dh[:, k, cols].bitcast(F32), ALU.mult, ALU.subtract, a)
            free[b] = d
            return d

        def xpose(src, t, dh, dl, gain, ready, *freed):
            return [xpose_half(src, t, half, dh, dl, gain, ready[half], *freed) for half in range(2)]

        nhalf = sb("nhalf", [P, T])
        nhalf_t = pool.do(lambda e: e.memset(nhalf[:, :], -0.5))
        rstd = st[:, 0:2]
        ss = st[:, 2:4]
        x_ready = [[None, None], [None, None]]
        x_used = [None]
        y_used = [None]
        h_ready = [[None, None], [None, None]]
        rstd_ready = [None, None]
        rstd_used = [None, None]
        junk = AR[:, 13056:14080]
        junk_used = [None]

        def norm(t, name):
            x_ready[t] = xpose(h[:, t, :], t, xh, xl, lambda k: parm(name, k), h_ready[t], x_used[0])
            a = A(junk, h[:, t, :], ACT.Square, *h_ready[t], junk_used[0], accum=ss[:, t:t + 1])
            junk_used[0] = a
            rstd_ready[t] = rsqrt(rstd[:, t:t + 1], ss[:, t:t + 1], D, a, rstd_used[t])

        def in_chunk(evac, second=None, banks=(4, 5), lhs=None):
            us = take(2)
            lh, ll, ready = lhs or (xh, xl, x_ready)
            for t in range(2):
                b = banks[t]
                pe.wait(free[b])
                for j, u in enumerate(us):
                    pe.wait(lo_done[u], ready[t][j])
                    for k in range(4):
                        kk = 4 * j + k
                        tok = mm3(ps[b][:, :], lh[:, kk, P * t:P * t + P], ll[:, kk, P * t:P * t + P],
                                  whi[:, u % S, 512 * k:512 * k + 512], wlo[:, u % S, 512 * k:512 * k + 512],
                                  kk == 0, kk == 7, inc=k == 3)
                    if t == 1:
                        unit_done[u] = tok
                    if j == 1:
                        evac(t, b, tok)
                    if second and t == 0 and j == 0:
                        second()
                    gap()
                    if t == 1 and j == 0:
                        pump()
            return tok

        def out_part(u, t, k0, lh, ll, ready, first, last):
            pe.wait(lo_done[u], ready[t])
            if first:
                pe.wait(free[2 * t], free[2 * t + 1])
            for k in range(2):
                lhs = [x[:, k0 + k, P * t:P * t + P] for x in (lh, ll)]
                for half in range(2):
                    c = 1024 * k + 512 * half
                    tok = mm3(ps[2 * t + half][:, :], lhs[0], lhs[1], whi[:, u % S, c:c + 512],
                              wlo[:, u % S, c:c + 512], first and k == 0, last and k == 1,
                              inc=k == 1 and half == 1)
            if t == 1:
                unit_done[u] = tok
            return tok

        def out_unit(k0, lh, ll, ready, first):
            u, = take(1)
            for t in range(2):
                tok = out_part(u, t, k0, lh, ll, ready, first, False)
            return tok

        def out_last(k0s, lh, ll, readies, weight, following):
            us = take(2)
            for n in range(2):
                tok = out_part(us[n], 0, k0s[n], lh, ll, readies[n], False, n == 1)
            residual(0, tok, weight)
            out_part(us[0], 1, k0s[0], lh, ll, readies[0], False, False)
            if following:
                norm(0, following)
            tok = out_part(us[1], 1, k0s[1], lh, ll, readies[1], False, True)
            residual(1, tok, weight)
            return tok

        def residual(t, tok, weight=1.0):
            for half in range(2):
                cols = slice(512 * half, 512 * half + 512)
                b = 2 * t + half
                if weight == 1.0:
                    d = TT(h[:, t, cols], ps[b][:, :], h[:, t, cols], ALU.add, tok, h_ready[t][half])
                else:
                    d = STT(h[:, t, cols], ps[b][:, :], weight, h[:, t, cols], ALU.mult, ALU.add, tok,
                            h_ready[t][half])
                h_ready[t][half] = free[b] = d

        def square_out(lh, ll, ready, following):
            r = [[ready[0][n], ready[1][n]] for n in range(2)]
            for n in range(2):
                out_unit(2 * n, lh, ll, r[0], n == 0)
            return out_last((4, 6), lh, ll, (r[1], r[1]), 1.0, following)

        def ffn(name, weight, following):
            ht_ready = {}
            hid_read = [None, None]
            sil_read = [None, None]
            down_done = {}

            def evac(j):
                def f(t, b, tok):
                    a = A(sil[:, t, :], ps[b][:, 0:256], ACT.Silu, tok, rstd_ready[t], sil_read[t],
                          scale=rstd[:, t:t + 1])
                    d = STT(hid[:, t, :], ps[b][:, 256:512], rstd[:, t:t + 1], sil[:, t, :], ALU.mult, ALU.mult,
                            a, hid_read[t])
                    free[b] = sil_read[t] = rstd_used[t] = d
                    hid_done[t] = d
                return f

            def turn(j):
                b = tbank()
                for t in range(2):
                    for k in range(2):
                        tok = tr(ps[b][:, 256 * k + P * t:256 * k + P * t + P], hid[:, t, P * k:P * k + P],
                                 (hid_done[t], free[b]), inc=k == 1)
                    hid_read[t] = tok
                k0 = 2 * (j % 4)
                a = A(yh[:, k0:k0 + 2, :], ps[b][:, :].rearrange("p (k c) -> p k c", k=2), ACT.Copy, tok,
                      down_done.get(j - 4), y_used[0])
                d = TT(yl[:, k0:k0 + 2, :], ps[b][:, :].rearrange("p (k c) -> p k c", k=2),
                       yh[:, k0:k0 + 2, :].bitcast(F32), ALU.subtract, a)
                free[b] = ht_ready[j] = d

            def down(j):
                down_done[j] = out_unit(2 * (j % 4), yh, yl, [ht_ready[j]] * 2, j == 0)

            def down(j):
                down_done[j] = out_unit(2 * (j % 4), yh, yl, [ht_ready[j]] * 2, j == 0)

            hid_done = [None, None]
            for j in range(FC):
                if j:
                    later(0, lambda: turn(j - 1))
                x_tok = in_chunk(evac(j), second=(lambda: norm(1, name)) if j == 0 else None)
                if 0 < j < FC - 2:
                    down(j - 1)
            x_used[0] = x_tok
            down(FC - 3)
            turn(FC - 1)
            j = FC - 2
            y_used[0] = out_last([2 * (i % 4) for i in (j, j + 1)], yh, yl, [[ht_ready[i]] * 2 for i in (j, j + 1)],
                                 weight, following)

        def ar(start, *shape):
            n = 1
            for s in shape:
                n *= s
            v = AR[:, start:start + n]
            names = "abcd"[:len(shape)]
            if len(shape) > 1:
                v = v.rearrange(f"p ({' '.join(names)}) -> p {' '.join(names)}",
                                **{c: s for c, s in zip(names, shape)})
            return v

        tok_x = [load(h[:, t, :], xin[t]) for t in range(2)]
        tok_k = load(kc[:, :], cst)
        tok_p = load(pr[:, :], par)
        while load_unit():
            pass
        for t in range(2):
            h_ready[t] = [tok_x[t], tok_x[t]]
        pe.wait(tok_k)
        dve.wait(tok_p, tok_k)
        act.wait(tok_p, tok_k)
        pool.wait(tok_k)

        wgr = ar(0, 128)
        wg2s = AR[0:16, 128:384]
        bg = ar(384, 256)
        tok_wg = load(wgr, wg)
        tok_wg2 = load(wg2s, wg2)
        tok_bg = load(bg, brow["b_gate"])
        gqn = ar(640, 2, 512)
        gvn = ar(1664, 2, 512)
        srn = ar(2688, 2, 512)
        svn = ar(3712, 2, 512)
        sqn = ar(4736, 2, 512)
        sqT = ar(5760, 4, T)
        skT = ar(6784, 4, T)
        tmp = ar(7808, 2, 512)
        mixn = ar(8832, 2, D)
        gqT = ar(10880, 2, T)
        la = ar(11392, 2, T)
        zt = ar(11904, 3, 384)
        wgh = sb("wgh", [P, 128], F32R)
        wgl = sb("wgl", [P, 128], F32R)
        g_a = act.do(lambda e: e.copy(wgh[:, :], wgr), tok_wg)
        g_d = TT(wgl[:, :], wgr, wgh[:, :].bitcast(F32), ALU.subtract, g_a)
        gq8 = st[:, 4:5]
        gq8_t = TS(gq8, parm("gq"), 0.125, None, ALU.mult, None)

        read = {}

        def heads_evac(dst, gain, gain_tok, key):
            def f(t, b, tok):
                a = A(sqn[:, t, :], ps[b][:, :], ACT.Copy, tok, rstd_ready[t], read.get(("sqn", t)),
                      scale=rstd[:, t:t + 1])
                free[b] = a
                q3 = sqn[:, t, :].rearrange("p (h d) -> p h d", h=8)
                t3 = tmp[:, t, :].rearrange("p (h d) -> p h d", h=8)
                s8 = st[:, 8 + 8 * t:16 + 8 * t]
                d = TT(tmp[:, t, :], sqn[:, t, :], sqn[:, t, :], ALU.mult, a, read.get(("tmp", t)))
                d = dve.do(lambda e: e.tensor_reduce(s8, t3, AXX, ALU.add), d)
                d = rsqrt(s8, s8, 64, d)
                d = TT(t3, q3, s8.unsqueeze(2).to_broadcast([P, 8, 64]), ALU.mult, d)
                read[("sqn", t)] = d

                def turned():
                    b2 = tbank()
                    for i in range(4):
                        tk = tr(ps[b2][:, P * i:P * i + P], tmp[:, t, P * i:P * i + P], (d, free[b2]), inc=i == 3)
                    read[("tmp", t)] = tk
                    free[b2] = key[t] = A(dst[:, :, P * t:P * t + P],
                                          ps[b2][:, :].rearrange("p (k c) -> p k c", k=4), ACT.Copy, tk, gain_tok,
                                          scale=gain)
                later(2 if t == 0 else 1, turned)
            return f

        def plain(dst, key, func=ACT.Copy):
            def f(t, b, tok):
                free[b] = key[t] = A(dst[:, t, :], ps[b][:, :], func, tok, rstd_ready[t], scale=rstd[:, t:t + 1])
            return f

        sq_t, sk_t, sv_t, gqk_t, gv_t, gr_t = ([None, None] for _ in range(6))
        norm(0, "mix0")
        pump()
        in_chunk(heads_evac(sqT, gq8, gq8_t, sq_t), second=lambda: norm(1, "mix0"))
        in_chunk(heads_evac(skT, parm("gk"), None, sk_t))

        glr = ar(13056, 2, 16)
        glT = AR[0:16, 13088:13344]
        la2 = la.rearrange("p a b -> p (a b)")
        e1 = ar(7808, 512)
        gl = {}

        def gate_rank():
            b = tbank()
            pe.wait(free[b], g_d)
            for t in range(2):
                for k in range(8):
                    tok = mm3(ps[b][:, 16 * t:16 * t + 16], xh[:, k, P * t:P * t + P], xl[:, k, P * t:P * t + P],
                              wgh[:, 16 * k:16 * k + 16], wgl[:, 16 * k:16 * k + 16], k == 0, k == 7, inc=k == 7)
            for t in range(2):
                a = A(glr[:, t, :], ps[b][:, 16 * t:16 * t + 16], ACT.Copy, tok, junk_used[0], scale=rstd[:, t:t + 1])
            free[b] = gl["glr"] = a

        def gate_turn():
            b = tbank()
            for t in range(2):
                tok = tr(ps[b][0:16, P * t:P * t + P], glr[:, t, :], (gl["glr"], free[b]), inc=t == 1)
            free[b] = gl["glT"] = A(glT, ps[b][0:16, 0:256], ACT.Copy, tok)

        def gate_log():
            b = tbank()
            pe.wait(gl["glT"], tok_wg2, free[b])
            for t in range(2):
                tok = mm(ps[b][:, 256 * t:256 * t + 256], glT[:, P * t:P * t + P], wg2s, inc=t == 1)
            d = dve.do(lambda e: e.tensor_tensor(la, ps[b][:, :].rearrange("p (a c) -> p a c", a=2),
                                                 bg.unsqueeze(1).to_broadcast([P, 2, 256]), ALU.add), tok, tok_bg)
            free[b] = d
            a = A(e1, la2, ACT.Abs, d, *[read[("tmp", t)] for t in range(2)])
            a = A(e1, e1, ACT.Exp, a, scale=-1.0)
            a = A(e1, e1, ACT.Ln, a, bias=1.0)
            gl["la"] = STT(la2, la2, 0.0, e1, ALU.min, ALU.subtract, a)

        def decays():
            b = tbank()
            pe.wait(free[b], gl["la"])
            for t in range(2):
                tok = mm(ps[b][:, 256 * t:256 * t + 256], const("rest"), la[:, t, :], inc=t == 1)
            gl["e"] = free[b] = A(e1, ps[b][:, :], ACT.Exp, tok, gl["la"], scale=1.0 / 16)
            b = tbank()
            pe.wait(free[b])
            for j in range(2):
                for t in range(2):
                    c = 4 * j + 2 * t
                    tok = mm(ps[b][:, c:c + 2], la[:, t, P * j:P * j + P], const("blk", 2), inc=j == 1 and t == 1)
            gl["dec"] = free[b] = A(st[:, 24:32], ps[b][:, 0:8], ACT.Exp, tok, scale=1.0 / 16)

        mask2 = const("mask", 256).rearrange("p (a c) -> p a c", a=2)
        bufs = [(zt[:, 0, :], zt[:, 1, :], zt[:, 2, :]),
                (ar(4736, 384), ar(5120, 384), ar(13344, 384))]
        zr = {}

        def z_scores(i):
            pr0, j = 64 * (i % 2), i // 2
            kT, qT = skT[pr0:pr0 + 64, j, :], sqT[pr0:pr0 + 64, j, :]
            z = ps[0]
            pe.wait(free[0], *sq_t, *sk_t)
            mm(z[:, 0:256], kT[:, 0:128], qT[:, 0:256], inc=False)
            tok = mm(z[:, 256:384], kT[:, 128:256], qT[:, 128:256])
            ls, kp, w = bufs[i % 2]
            a = A(w, z[:, 0:384], ACT.Abs, tok, zr.get(("w", i - 2)), *[read[("sqn", t)] for t in range(2)])
            a = A(w, w, ACT.Exp, a, scale=-1.0)
            a = A(w, w, ACT.Ln, a, bias=1.0)
            d = STT(ls, z[:, 0:384], 0.0, w, ALU.min, ALU.subtract, a, zr.get(("ls", i - 2)))
            d = TT(kp, ls, z[:, 0:384], ALU.subtract, d, zr.get(("kp", i - 2)))
            free[0] = d
            kd = kp.rearrange("p (a c) -> p a c", a=3)[:, 0:3:2, :]
            zr[("keep", i)] = TT(kd, kd, mask2, ALU.mult, d)

        def z_between(i):
            ls, kp, w = bufs[i % 2]
            bt = ps[1]
            pe.wait(free[1], zr[("keep", i)])
            mm(bt[:, 0:256], const("later"), kp[:, 0:256], start=True, stop=False, skip=True, inc=False)
            mm(bt[:, 128:256], const("ones"), kp[:, 256:384], start=False, stop=False, skip=True, inc=False)
            tok = mm(bt[:, 256:384], const("later"), kp[:, 256:384], start=False, stop=True, skip=True)
            zr[("kp", i)] = tok
            d = TT(w, ls, bt[:, 0:384], ALU.add, tok)
            free[1] = zr[("ls", i)] = d
            a = A(w, w, ACT.Exp, d)
            wd = w.rearrange("p (a c) -> p a c", a=3)[:, 0:3:2, :]
            zr[("weights", i)] = TT(wd, wd, mask2, ALU.mult, a)

        def z_values(i):
            ls, kp, w = bufs[i % 2]
            pe.wait(free[2], free[3], zr[("weights", i)], *sv_t)
            hc = slice(64 * i, 64 * i + 64)
            mm(ps[2][:, hc], w[:, 0:128], svn[:, 0, hc], inc=False)
            mm(ps[3][:, hc], w[:, 128:256], svn[:, 0, hc], start=True, stop=False, inc=False)
            zr[("w", i)] = mm(ps[3][:, hc], w[:, 256:384], svn[:, 1, hc], start=False, stop=True)

        def turn_q():
            b = tbank()
            for j in range(2):
                for t in range(2):
                    c = 256 * j + P * t
                    tok = tr(ps[b][:, c:c + P], gqn[:, t, P * j:P * j + P], (gqk_t[t], free[b]),
                             inc=j == 1 and t == 1)
            gl["q"] = free[b] = A(gqT, ps[b][:, :].rearrange("p (j c) -> p j c", j=2), ACT.Copy, tok, scale=0.125)

        def keys():
            e3 = e1.rearrange("p (t c) -> p t c", t=2)
            gl["k"] = TT(gqn[:, :, 256:512], gqn[:, :, 256:512], e3, ALU.mult, gl["e"], *gqk_t)

        sts = [sb(f"state{n}", [P, 2, 256]) for n in range(2)]
        zer = [pool.do(lambda e, n=n: e.memset(sts[n][:, :, :], 0.0)) for n in range(2)]
        o_done, s_done, g_done = {}, {}, {}

        def state(n):
            t, c = divmod(n, 2)
            rows = slice(64 * c, 64 * c + 64)
            ub = tbank()
            pe.wait(free[ub], gl["k"], *gv_t)
            for j in range(2):
                tok = mm(ps[ub][:, 256 * j:256 * j + 256], gqn[rows, t, 256 + P * j:256 + P * j + P],
                         gvn[rows, t, 256 * j:256 * j + 256], inc=j == 1)
            cur, prev = sts[n % 2], sts[(n + 1) % 2]
            for g in range(2):
                rr, cc = slice(64 * g, 64 * g + 64), slice(P * g, P * g + P)
                for j in range(2):
                    uu = ps[ub][rr, 256 * j + P * g:256 * j + P * g + P]
                    if n == 0:
                        d = dve.do(lambda e, o=cur[rr, j, cc], i=uu: e.tensor_copy(o, i), tok, *zer)
                    else:
                        d = STT(cur[rr, j, cc], prev[rr, j, cc], st[rr, 24 + 4 * j + n:25 + 4 * j + n], uu,
                                ALU.mult, ALU.add, tok, gl["dec"], o_done.get(n - 2), s_done.get(n - 1))
            s_done[n] = free[ub] = d

        def queried(n):
            t, c = divmod(n, 2)
            rows = slice(64 * c, 64 * c + 64)
            ob = tbank()
            pe.wait(s_done[n], gl["q"], free[ob])
            for j in range(2):
                o_done[n] = mm(ps[ob][rows, 256 * j:256 * j + 256], gqT[:, j, 64 * n:64 * n + 64],
                               sts[n % 2][:, j, :], inc=j == 1)
            g_done[n] = free[ob] = A(mixn[rows, t, 0:512], ps[ob][rows, :], ACT.Copy, o_done[n])

        steps = [[] for _ in range(22)]
        for i in range(8):
            steps[2 * i].append(lambda i=i: z_scores(i))
            steps[2 * i + 2].append(lambda i=i: z_between(i))
            steps[2 * i + 3].append(lambda i=i: z_values(i))
        steps[1].append(gate_rank)
        steps[2].append(gate_turn)
        steps[3].append(gate_log)
        steps[5].append(decays)
        steps[8].append(turn_q)
        steps[9].append(keys)
        for n in range(4):
            steps[12 + n].append(lambda n=n: state(n))
            steps[13 + n].append(lambda n=n: queried(n))
        for n, fns in enumerate(steps):
            for fn in fns:
                later(n + 1, fn)
        in_chunk(plain(svn, sv_t))
        in_chunk(plain(gqn, gqk_t))
        in_chunk(plain(gvn, gv_t))
        x_used[0] = in_chunk(plain(srn, gr_t, ACT.Silu))
        gaps_left()

        y_ready = [None, None]
        gla_out = [None, None]
        for t in range(2):
            m = mixn[:, t, 0:512]
            m3 = m.rearrange("p (h d) -> p h d", h=4)
            tp = tmp[:, t, :]
            tp3 = tp.rearrange("p (h d) -> p h d", h=4)
            s4 = st[:, 32 + 4 * t:36 + 4 * t]
            d = TT(tp, m, m, ALU.mult, g_done[2 * t], g_done[2 * t + 1], gl["k"])
            d = dve.do(lambda e, s4=s4, tp3=tp3: e.tensor_reduce(s4, tp3, AXX, ALU.add), d)
            gla_out[t] = rsqrt(s4, s4, 128, d)
        for t in range(2):
            m = mixn[:, t, 0:512]
            m3 = m.rearrange("p (h d) -> p h d", h=4)
            s4 = st[:, 32 + 4 * t:36 + 4 * t]
            d = TT(m3, m3, s4.unsqueeze(2).to_broadcast([P, 4, 128]), ALU.mult, gla_out[t])
            gla_out[t] = TT(m, m, srn[:, t, :], ALU.mult, d, gr_t[t])
        for t in range(2):
            free[2 + t] = A(mixn[:, t, 512:1024], ps[2 + t][:, :], ACT.Copy, zr[("w", 7)])
        y_ready = [[xpose_half(mixn[:, t, :], t, 0, yh, yl, lambda k: parm("gla"), gla_out[t], y_used[0]), None]
                   for t in range(2)]
        for t in range(2):
            y_ready[t][1] = xpose_half(mixn[:, t, :], t, 1, yh, yl, lambda k: None, free[2 + t], y_used[0])
        y_used[0] = square_out(yh, yl, y_ready, "ffn0")

        arena_free = [y_used[0], list(free)]
        ffn("ffn0", 1.0, "mix1")

        ND, NP_ = 5, 3
        bp1 = ar(0, 2048)
        bp2 = ar(2048, 1024)
        t_bp1 = load(bp1, brow["b_pw1"], *arena_free)
        t_bp2 = load(bp2, brow["b_pw2"])
        glu = ar(3072, 2, 512)
        upad = ar(4096, 8, 286)
        cv = ar(6384, 8, T)
        sq = ar(8432, 8, T)
        mu = ar(10480, T)
        dg = ar(10736, 2, P)
        u2 = ar(10992, 2, 256)
        wlow = ar(11504, 31 * NP_)
        wdh = sb("wdh", [P, 31 * NP_], F32R)
        z0 = pool.do(lambda e: e.memset(upad[:, :, 0:30], 0.0), *arena_free)
        gl_read, gl_done, up_t = {}, [None, None], [None] * 8
        cvt = [None] * 8

        wd_a = act.do(lambda e: e.copy(wdh[:, :], parm("w_dw", 31 * ND, 31 * NP_)))
        wd_d = TT(wlow, parm("w_dw", 31 * ND, 31 * NP_), wdh[:, :].bitcast(F32), ALU.subtract, wd_a, *arena_free)
        NDG = 16
        diag_t, diag_used, diag_next = {}, {}, [0]

        def diagonals():
            while diag_next[0] < 31 * NP_ and (diag_next[0] < NDG or diag_next[0] - NDG in diag_used):
                n = diag_next[0]
                o = (slice(None), (n % NDG) // 2, slice(P * (n % 2), P * (n % 2) + P))
                diag_next[0] += 1
                f = diag_used.get(n - NDG)
                a = A(yh[o], ident, ACT.Copy, wd_a, f, y_used[0], scale=wdh[:, n:n + 1].bitcast(F32))
                c = TS(yl[o], ident, wlow[:, n:n + 1], 1.0, ALU.mult, ALU.mult, wd_d, f, y_used[0], eng=pool)
                diag_t[n] = [a, c]

        def glu_evac(j):
            def f(t, b, tok):
                ga, gb = glu[:, t, 0:256], glu[:, t, 256:512]
                bias = bp1[:, 512 * j:512 * j + 512]
                d = STT(glu[:, t, :], ps[b][:, :], rstd[:, t:t + 1], bias, ALU.mult, ALU.add, tok, t_bp1,
                        rstd_ready[t])
                free[b] = rstd_used[t] = d
                a = A(gb, gb, ACT.Sigmoid, d)
                gl_done[t] = TT(u2[:, t, :], ga, gb, ALU.mult, a, gl_read.get(t))
            return f

        def glu_turn(j):
            b = tbank()
            for t in range(2):
                for k in range(2):
                    tok = tr(ps[b][:, 256 * k + P * t:256 * k + P * t + P], u2[:, t, P * k:P * k + P],
                             (gl_done[t], free[b]), inc=k == 1)
                gl_read[t] = tok
            a = A(upad[:, 2 * j:2 * j + 2, 30:286], ps[b][:, :].rearrange("p (k c) -> p k c", k=2), ACT.Copy, tok, z0)
            free[b] = up_t[2 * j] = up_t[2 * j + 1] = a

        def taps(c, lo, hi):
            for w in range(lo, hi):
                if w == 0:
                    d = TS(cv[:, c, :], upad[:, c, 0:256], parm("w_dw", 31 * c), parm("b_dw", c), ALU.mult, ALU.add,
                           up_t[c], z0)
                else:
                    d = STT(cv[:, c, :], upad[:, c, w:w + 256], parm("w_dw", 31 * c + w), cv[:, c, :], ALU.mult,
                            ALU.add, cvt[c])
                cvt[c] = d

        todo = [(c, w) for c in range(ND) for w in range(31)]

        def some_taps(n, most):
            while n and todo and todo[0][0] < most and up_t[todo[0][0]]:
                c, w = todo.pop(0)
                taps(c, w, w + 1)
                n -= 1

        diagonals()
        for j in range(4):
            if j:
                later(0, lambda j=j: glu_turn(j - 1))
                for g in range(4):
                    later(g, lambda j=j: some_taps(6, 2 * j))
            tokc = in_chunk(glu_evac(j), second=(lambda: norm(1, "mix1")) if j == 0 else None)
        x_used[0] = tokc
        glu_turn(3)

        xf = [x[:, :, :].rearrange("p k c -> p (k c)") for x in (xh, xl)]
        uh, ul = (x[:, 0:286 * NP_].rearrange("p (k c) -> p k c", k=NP_) for x in xf)
        uview = upad[:, ND:8, :]
        a = A(uh, uview, ACT.Copy, up_t[7], z0, tokc)
        u_t = TT(ul, uview, uh.bitcast(F32), ALU.subtract, a)
        cb = [ps[4], ps[5], ps[0]]
        cbi = [4, 5, 0]
        for n in range(31 * NP_):
            c, w = divmod(n, 31)
            if w == 0:
                pe.wait(u_t, free[cbi[c]])
            pe.wait(*diag_t[n])
            o = (slice(None), (n % NDG) // 2, slice(P * (n % 2), P * (n % 2) + P))
            diag_used[n] = mm3(cb[c][:, 0:256], yh[o], yl[o], uh[:, c, w:w + 256], ul[:, c, w:w + 256], w == 0,
                               w == 30, inc=True)
            diagonals()
            if n % 2:
                some_taps(4 if n % 4 == 1 else 3, ND)
            if w == 30:
                a = A(cv[:, ND + c, :], cb[c][:, 0:256], ACT.Identity, diag_used[n], bias=parm("b_dw", ND + c))
                free[cbi[c]] = cvt[ND + c] = a
        some_taps(1000, ND)
        y_used[0] = diag_used[31 * NP_ - 1]

        pe.wait(free[1])
        order = [0, 1, 2, 3, 5, 6, 7, 4]
        for n, c in enumerate(order):
            tok = mm(ps[1][:, 0:256], const("ones"), cv[:, c, :], start=n == 0, stop=n == 7, deps=(cvt[c],),
                     inc=n == 7)
        a = A(mu, ps[1][:, 0:256], ACT.Copy, tok, scale=1.0 / D)
        free[1] = a
        mub = mu.unsqueeze(1).to_broadcast([P, 4, T])
        sqd = []
        for half in range(2):
            cs = slice(4 * half, 4 * half + 4)
            d = TT(cv[:, cs, :], cv[:, cs, :], mub, ALU.subtract, a)
            sqd.append(A(sq[:, cs, :], cv[:, cs, :], ACT.Square, d))
        pe.wait(free[2])
        for t in range(2):
            for c in range(8):
                tok = mm(ps[2][:, t:t + 1], sq[:, c, P * t:P * t + P], const("ones", 1), start=c == 0, stop=c == 7,
                         deps=(sqd[c // 4],), inc=c == 7)
        d = TS(st[:, 48:50], ps[2][:, 0:2], 1.0 / D, EPS, ALU.mult, ALU.add, tok)
        free[2] = d
        d = TT(st[:, 48:50], st[:, 48:50], nhalf[:, 0:2], ALU.pow, d, eng=pool)
        for t in range(2):
            d1 = TS(dg[:, t, :], ident, st[:, 48 + t:49 + t], 1.0, ALU.mult, ALU.mult, d)
        pe.wait(free[3])
        tok = mm(ps[3][:, 0:256], const("ones"), dg.rearrange("p t c -> p (t c)"), deps=(d1,))
        done = []
        rsb = ps[3][:, 0:256].unsqueeze(1).to_broadcast([P, 2, T])
        for g in range(4):
            cs = slice(2 * g, 2 * g + 2)
            d = TT(cv[:, cs, :], cv[:, cs, :], rsb, ALU.mult, tok)
            for c in (2 * g, 2 * g + 1):
                a = A(cv[:, c, :], cv[:, c, :], ACT.Silu, d, scale=parm("ln_g", c), bias=parm("ln_b", c))
            a = A(yh[:, cs, :], cv[:, cs, :], ACT.Copy, a, y_used[0])
            done.append((a, cs))
        free[3] = d
        done = [TT(yl[:, cs, :], cv[:, cs, :], yh[:, cs, :].bitcast(F32), ALU.subtract, a, y_used[0])
                for a, cs in done]
        for t in range(2):
            for half in range(2):
                cols = slice(512 * half, 512 * half + 512)
                h_ready[t][half] = TT(h[:, t, cols], h[:, t, cols], bp2[:, cols], ALU.add, h_ready[t][half], t_bp2,
                                      x_ready[t], junk_used[0])
        y_used[0] = square_out(yh, yl, [[done[1], done[3]]] * 2, "ffn1")

        arena_free = [y_used[0], list(free)]
        ffn("ffn1", 1.0, "n1")
        ffn("n1", 0.5, "nm")

        gb = ar(0, 2048)
        cosn = ar(2048, 2, 2, 128)
        rm = ar(2560, 4, 384)
        pm = ar(4096, 4, 384)
        t_gb = load(gb, brow["gate_bias"], *arena_free)
        t_cs = load(cosn.rearrange("p a b c -> p (a b c)"), cosin)
        t_rm = load(rm.rearrange("p a b -> p (a b)"), rmask)
        t_pm = load(pm.rearrange("p a b -> p (a b)"), pmat)
        merged = ar(5632, 2, D)
        qT = ar(7680, 4, T)
        kT = ar(8704, 4, T)
        sig0 = ar(7680, 2, D)
        vn = ar(9728, 2, 1024)
        pn = ar(9728, 2, 1024)
        ro = ar(11776, 2, 512)
        sc = [ar(12800, 384), ar(13696, 384)]
        gt = ar(13184, 512)
        rtmp = ar(13184, 256)

        p_t = [[None, None], [None, None]]

        def p_evac(j):
            def f(t, b, tok):
                free[b] = p_t[j][t] = A(pn[:, t, 512 * j:512 * j + 512], ps[b][:, :], ACT.Copy, tok, rstd_ready[t],
                                        scale=rstd[:, t:t + 1])
            return f

        pl_ready, pn_read = {}, [None]

        def pooled(g):
            b = tbank()
            pe.wait(free[b], *p_t[g // 2], t_pm)
            for c in (2 * g, 2 * g + 1):
                o = 256 * (c % 2)
                cols = slice(P * c, P * c + P)
                mm(ps[b][:, o:o + 256], pn[:, 0, cols], pm[:, g, 0:256], start=c % 2 == 0, stop=False, skip=True,
                   inc=False)
                tok = mm(ps[b][:, o + 128:o + 256], pn[:, 1, cols], pm[:, g, 256:384], start=False, stop=True,
                         skip=True)
            src = ps[b][:, :].rearrange("p (k c) -> p k c", k=2)
            a = A(yh[:, 2 * g:2 * g + 2, :], src, ACT.Copy, tok, y_used[0])
            d = TT(yl[:, 2 * g:2 * g + 2, :], src, yh[:, 2 * g:2 * g + 2, :].bitcast(F32), ALU.subtract, a)
            free[b] = pl_ready[g] = d
            pn_read[0] = tok

        sg_t = {}

        def gate_evac(which, j, dst, *freed):
            def f(t, b, tok):
                g_ = dst[:, t, 512 * j:512 * j + 512]
                d = STT(g_, ps[b][:, :], rstd[:, t:t + 1], gb[:, 1024 * which + 512 * j:1024 * which + 512 * j + 512],
                        ALU.mult, ALU.add, tok, rstd_ready[t], t_gb, *freed)
                free[b] = rstd_used[t] = d
                sg_t[(which, j, t)] = A(g_, g_, ACT.Sigmoid, d)
            return f

        mg_t = {}

        def pool_evac(j):
            def f(t, b, tok):
                m = merged[:, t, 512 * j:512 * j + 512]
                free[b] = mg_t[(j, t)] = TT(m, ps[b][:, :], m, ALU.mult, tok, sg_t[(1, j, t)])
            return f

        def merge_evac(j):
            def f(t, b, tok):
                m = merged[:, t, 512 * j:512 * j + 512]
                s_ = sig0[:, t, 512 * j:512 * j + 512]
                d = free[b] = TT(s_, ps[b][:, :], s_, ALU.mult, tok, sg_t[(0, j, t)])
                mg_t[(j, t)] = TT(m, m, s_, ALU.add, d, mg_t[(j, t)])
            return f

        for j in range(2):
            in_chunk(p_evac(j), second=(lambda: norm(1, "nm")) if j == 0 else None)
        later(0, lambda: pooled(0))
        later(1, lambda: pooled(1))
        later(2, lambda: pooled(2))
        later(3, lambda: pooled(3))
        for j in range(2):
            in_chunk(gate_evac(1, j, merged))
        u, = take(1)
        pe.wait(lo_done[u])
        for g in range(4):
            pe.wait(free[g], pl_ready[g])
            for dd in range(2):
                for cc in range(2):
                    c = 512 * g + 256 * cc + P * dd
                    tok = mm3(ps[g][:, 256 * dd:256 * dd + 256], whi[:, u % S, c:c + P], wlo[:, u % S, c:c + P],
                              yh[:, 2 * g + cc, :], yl[:, 2 * g + cc, :], cc == 0, cc == 1, inc=cc == 1)
            pl_ready[g] = tok
        unit_done[u] = tok
        pool_ready = []
        for g in range(4):
            for k in (2 * g, 2 * g + 1):
                a = A(yh[:, k, :], ps[g][:, 256 * (k % 2):256 * (k % 2) + 256], ACT.Copy, pl_ready[g],
                      scale=parm("pool", k))
            for k in (2 * g, 2 * g + 1):
                d = STT(yl[:, k, :], ps[g][:, 256 * (k % 2):256 * (k % 2) + 256], parm("pool", k),
                        yh[:, k, :].bitcast(F32), ALU.mult, ALU.subtract, a)
            free[g] = d
            pool_ready.append(d)
        pool_r = [[pool_ready[1], pool_ready[3]]] * 2

        ro_read, rt_read, tr_read = [None, None], [None], [None]
        v_t = [[None, None], [None, None]]

        def v_evac(j):
            def f(t, b, tok):
                free[b] = v_t[j][t] = A(vn[:, t, 512 * j:512 * j + 512], ps[b][:, :], ACT.Copy, tok, rstd_ready[t],
                                        pn_read[0], scale=rstd[:, t:t + 1])
            return f

        def rot_evac(dst, ready):
            def f(t, b, tok):
                x = ps[b][:, :].rearrange("p (h a d) -> p h a d", h=2, a=2)
                o = ro[:, t, :].rearrange("p (h a d) -> p h a d", h=2, a=2)
                w = rtmp[:, :].rearrange("p (h d) -> p h d", h=2)
                cs_, sn = (cosn[:, t, i:i + 1, :].to_broadcast([P, 2, 128]) for i in range(2))
                r_ = rstd[:, t:t + 1]
                d1 = STT(o[:, :, 0, :], x[:, :, 0, :], r_, cs_, ALU.mult, ALU.mult, tok, rstd_ready[t], t_cs,
                         ro_read[t])
                d2 = STT(w, x[:, :, 1, :], r_, sn, ALU.mult, ALU.mult, rt_read[0])
                d1 = TT(o[:, :, 0, :], o[:, :, 0, :], w, ALU.subtract, d1, d2)
                d2 = STT(w, x[:, :, 0, :], r_, sn, ALU.mult, ALU.mult, d1)
                d3 = STT(o[:, :, 1, :], x[:, :, 1, :], r_, cs_, ALU.mult, ALU.mult)
                free[b] = d3
                d = TT(o[:, :, 1, :], o[:, :, 1, :], w, ALU.add, d3)
                rt_read[0] = d

                def turned():
                    b2 = tbank()
                    for i in range(4):
                        tk = tr(ps[b2][:, P * i:P * i + P], ro[:, t, P * i:P * i + P], (d, free[b2]), inc=i == 3)
                    ro_read[t] = tk
                    free[b2] = ready[t] = A(dst[:, :, P * t:P * t + P],
                                            ps[b2][:, :].rearrange("p (k c) -> p k c", k=4), ACT.Copy, tk,
                                            tr_read[0])
                later(2, turned)
            return f

        sc_t, pv_t = {}, {}
        ret_t = {}

        def ret_scores(i, q_r, k_r):
            hh = 2 * (i % 2)
            sb_ = i % 2
            pe.wait(free[sb_], *q_r, *k_r)
            for c in range(2):
                mm(ps[sb_][:, 0:256], kT[:, hh + c, 0:128], qT[:, hh + c, :], start=c == 0, stop=c == 1, inc=False)
            for c in range(2):
                tok = mm(ps[sb_][:, 256:384], kT[:, hh + c, 128:256], qT[:, hh + c, 128:256], start=c == 0,
                         stop=c == 1, inc=c == 1)
            tr_read[0] = tok
            d = TT(sc[sb_], ps[sb_][:, 0:384], rm[:, i, :], ALU.mult, tok, t_rm, pv_t.get(i - 2))
            free[sb_] = sc_t[i] = d

        def ret_values(i):
            vc = slice(256 * i, 256 * i + 256)
            s_ = sc[i % 2]
            pe.wait(sc_t[i], free[2], free[3], *v_t[i // 2])
            c0 = 256 * (i % 2)
            mm(ps[2][:, c0:c0 + 256], s_[:, 0:128], vn[:, 0, vc], inc=False)
            mm(ps[3][:, c0:c0 + 256], s_[:, 128:256], vn[:, 0, vc], start=True, stop=False, inc=False)
            pv_t[i] = mm(ps[3][:, c0:c0 + 256], s_[:, 256:384], vn[:, 1, vc], start=False, stop=True)

        def ret_norm(j):
            for t in range(2):
                v_ = vn[:, t, 512 * j:512 * j + 512]
                v3 = v_.rearrange("p (h d) -> p h d", h=2)
                a = A(v_, ps[2 + t][:, :], ACT.Copy, pv_t[2 * j + 1])
                free[2 + t] = a
                s2 = st[:, 50 + 4 * j + 2 * t:52 + 4 * j + 2 * t]
                r_ = (sil, hid)[t][:, :, :].rearrange("p a c -> p (a c)")
                d = TT(r_, v_, v_, ALU.mult, a)
                d = dve.do(lambda e, s2=s2, r3=r_.rearrange("p (h d) -> p h d", h=2): e.tensor_reduce(
                    s2, r3, AXX, ALU.add), d)
                d = rsqrt(s2, s2, 256, d)
                ret_t[(j, t)] = TT(v3, v3, s2.unsqueeze(2).to_broadcast([P, 2, 256]), ALU.mult, d)

        gt_read = [None]
        gs_t = {}

        def gret_evac(j):
            def f(t, b, tok):
                a = A(gt, ps[b][:, :], ACT.Silu, tok, rstd_ready[t], gt_read[0], rt_read[0], scale=rstd[:, t:t + 1])
                free[b] = a
                v_ = vn[:, t, 512 * j:512 * j + 512]
                gt_read[0] = gs_t[(j, t)] = TT(v_, v_, gt, ALU.mult, a, ret_t[(j, t)])
            return f

        def ret_turn(t, half):
            y_ready[t][half] = xpose_half(vn[:, t, :], t, half, yh, yl, lambda k: None, gs_t[(half, t)], y_used[0])

        in_chunk(v_evac(0))
        in_chunk(pool_evac(0), banks=(0, 1), lhs=(yh, yl, pool_r))
        y_used[0] = in_chunk(pool_evac(1), banks=(0, 1), lhs=(yh, yl, pool_r))
        in_chunk(v_evac(1))
        q_r, k_r = [None, None], [None, None]
        in_chunk(rot_evac(qT, q_r))
        in_chunk(rot_evac(kT, k_r))
        later(2, lambda: (ret_scores(0, q_r, k_r), ret_scores(1, q_r, k_r)))
        later(3, lambda: (ret_values(0), ret_values(1), ret_norm(0)))
        q_r2, k_r2 = [None, None], [None, None]
        in_chunk(rot_evac(qT, q_r2))
        in_chunk(rot_evac(kT, k_r2))
        later(2, lambda: (ret_scores(2, q_r2, k_r2), ret_scores(3, q_r2, k_r2)))
        later(3, lambda: (ret_values(2), ret_values(3), ret_norm(1)))
        in_chunk(gret_evac(0))
        y_ready = [[None, None], [None, None]]
        later(1, lambda: ret_turn(0, 0))
        later(2, lambda: ret_turn(1, 0))
        in_chunk(gret_evac(1))
        later(1, lambda: ret_turn(0, 1))
        later(2, lambda: ret_turn(1, 1))
        in_chunk(gate_evac(0, 0, sig0, tr_read[0]))
        x_used[0] = in_chunk(gate_evac(0, 1, sig0))
        in_chunk(merge_evac(0), banks=(0, 1), lhs=(yh, yl, y_ready))
        z_ready = [[None, None], [None, None]]

        def merged_turn(t, half):
            z_ready[t][half] = xpose_half(merged[:, t, :], t, half, xh, xl, lambda k: None, mg_t[(half, t)],
                                          x_used[0])

        later(1, lambda: merged_turn(0, 0))
        later(2, lambda: merged_turn(1, 0))
        y_used[0] = in_chunk(merge_evac(1), banks=(0, 1), lhs=(yh, yl, y_ready))
        us = take(2)
        for n in range(2):
            for t in range(2):
                out_part(us[n], t, 2 * n, xh, xl, [z_ready[0][0], z_ready[1][0]], n == 0, False)
            if n == 0:
                merged_turn(0, 1)
                merged_turn(1, 1)
        zr1 = [z_ready[0][1], z_ready[1][1]]
        x_held = x_used[0]
        us = take(2)
        for n in range(2):
            tok = out_part(us[n], 0, 4 + 2 * n, xh, xl, zr1, False, n == 1)
        residual(0, tok, 1.0)
        out_part(us[0], 1, 4, xh, xl, zr1, False, False)
        tok = out_part(us[1], 1, 6, xh, xl, zr1, False, True)
        x_used[0] = tok
        norm(0, "n2")
        residual(1, tok, 1.0)
        arena_free = [tok, list(free)]
        ffn("n2", 0.5, None)

        fin = ar(0, 1024)
        t_f = load(fin, brow["norm_final"], *arena_free)
        res = ar(1024, 2, D)
        stores = []
        for t in range(2):
            a = A(junk, h[:, t, :], ACT.Square, *h_ready[t], junk_used[0], accum=ss[:, t:t + 1])
            junk_used[0] = a
            d = rsqrt(rstd[:, t:t + 1], ss[:, t:t + 1], D, a, rstd_used[t])
            d = STT(res[:, t, :], h[:, t, :], rstd[:, t:t + 1], fin, ALU.mult, ALU.mult, d, t_f, arena_free)
            sem = ctx.enter_context(nc.semaphore(f"stored{t}"))
            sp.wait(d)
            sp.items.append(lambda e, t=t, sem=sem: e.dma_start(out[t], res[:, t, :]).then_inc(sem, 16))
            stores.append((sem, 16))
        sp.wait(*stores)
        assert at[0] == NU

        block = ctx.enter_context(nc.Block())

        @block.sync
        def _(e):
            for f in sp.items:
                f(e)

        @block.tensor
        def _(e):
            for f in pe.items:
                f(e)

        @block.scalar
        def _(e):
            for f in act.items:
                f(e)

        @block.vector
        def _(e):
            for f in dve.items:
                f(e)

        @block.gpsimd
        def _(e):
            for f in pool.items:
                f(e)


def constants():
    import numpy as np
    i = np.arange(128)
    cst = np.zeros((128, NKW), np.float32)
    cst[:, 0:128] = np.eye(128)
    cst[:, 128:256] = i[:, None] > i[None, :]
    cst[:, 256:384] = 1
    cst[:, 384:512] = cst[:, 512:640] = i[:, None] < i[None, :]
    cst[:, 640:768] = (i[:, None] > i[None, :]) & (i[:, None] // 64 == i[None, :] // 64)
    cst[:, 768:770] = i[:, None] // 64 == np.arange(2)[None, :]
    half = 128
    inv = (np.float32(10000.0) ** (-np.arange(half, dtype=np.float32) / np.float32(half))).astype(np.float32)
    ang = np.arange(256, dtype=np.float32)[:, None] * inv[None, :]
    cs = np.stack([np.cos(ang), np.sin(ang)], axis=1).astype(np.float32)
    cosin = np.ascontiguousarray(cs.reshape(2, 128, 2, 128).transpose(1, 0, 2, 3).reshape(128, 512))
    s = np.arange(256)
    rmask = np.zeros((128, 4, 384), np.float32)
    for g in range(4):
        gamma = 1.0 - 2.0 ** (-5.0 - g)
        m = np.where(s[:, None] // 64 <= s[None, :] // 64, gamma ** np.abs(s[:, None] - s[None, :]), 0.0) / 16.0
        rmask[:, g, 0:256] = m[0:128]
        rmask[:, g, 256:384] = m[128:256, 128:256]
    pmat = np.zeros((128, 4, 384), np.float32)
    for g, w in enumerate((2, 4, 8, 16)):
        d = s[None, :] - s[:, None]
        m = ((d >= 0) & (d < w)) / np.minimum(s[None, :] + 1.0, w) - (d == 0)
        pmat[:, g, 0:256] = m[0:128]
        pmat[:, g, 256:384] = m[128:256, 128:256]
    return cst, cosin, rmask.reshape(128, -1), pmat.reshape(128, -1)


def units_in(w):
    n = w.shape[1] // 512
    return w.reshape(2, 4, 128, n, 512).transpose(3, 0, 2, 1, 4).reshape(2 * n, 128, 2048)


def units_out(w):
    n = w.shape[0] // 256
    return w.reshape(n, 2, 128, 1024).transpose(0, 2, 1, 3).reshape(n, 128, 2048)


def units_ffn(wg, wu, wd):
    import numpy as np
    pair = np.stack([wg.reshape(1024, FC, 256), wu.reshape(1024, FC, 256)], axis=2).reshape(1024, FC * 512)
    a, b = units_in(pair), units_out(wd)
    seq = [a[0], a[1]]
    for j in range(1, FC - 2):
        seq += [a[2 * j], a[2 * j + 1], b[j - 1]]
    return seq + [*a[2 * FC - 4:], *b[FC - 3:]]


def layout(i):
    import numpy as np
    cst, cosin, rmask, pmat = constants()
    win = i["hy_w_in"][0]
    col = {}
    c = 0
    for n, w in (("gq", 256), ("gk", 256), ("gv", 512), ("gr", 512), ("glr", 16), ("sq", 512), ("sk", 512),
                 ("sv", 512)):
        col[n] = win[:, c:c + w]
        c += w
    seq = []
    for n in ("sq", "sk", "sv"):
        seq += list(units_in(col[n]))
    seq += list(units_in(np.concatenate([col["gq"], col["gk"]], axis=1)))
    seq += list(units_in(col["gv"])) + list(units_in(col["gr"]))
    seq += list(units_out(i["hy_w_out"][0]))
    seq += units_ffn(i["ffn_w_gate"][0], i["ffn_w_up"][0], i["ffn_w_down"][0])
    pw = i["cv_w_pw1"][0].reshape(1024, 2, 4, 256).transpose(0, 2, 1, 3).reshape(1024, 2048)
    seq += list(units_in(pw)) + list(units_out(i["cv_w_pw2"][0]))
    seq += units_ffn(i["ffn_w_gate"][1], i["ffn_w_up"][1], i["ffn_w_down"][1])
    f1 = i["ffn1_w_in_2"][0]
    seq += units_ffn(f1[:, :2816], f1[:, 2816:], i["ffn1_w_out_2"][0])
    w2 = i["w_in_2"][0]
    q, k, v, g, p = (w2[:, 1024 * n:1024 * n + 1024] for n in range(5))
    g0, g1 = w2[:, 5120:6144], w2[:, 6144:7168]
    v_ = units_in(v)
    seq += [*units_in(p), *units_in(g1)]
    seq.append(i["pool_w_2"][0].reshape(4, 2, 128, 256).transpose(2, 0, 1, 3).reshape(128, 2048))
    seq += [*v_[0:2], *units_in(i["w_pool_up_2"][0]), *v_[2:4]]
    a, b = units_in(q), units_in(k)
    seq += [*a[0:2], *b[0:2], *a[2:4], *b[2:4]]
    seq += [*units_in(g), *units_in(g0), *units_in(i["w_ret_up_2"][0])]
    seq += list(units_out(i["w_out_2"][0]))
    f2 = i["ffn2_w_in_2"][0]
    seq += units_ffn(f2[:, :2816], f2[:, 2816:], i["ffn2_w_out_2"][0])

    def cols(x):
        return x.reshape(-1, 128).T

    def twice(x):
        return np.concatenate([x, x]).reshape(128, 1)

    par = np.concatenate([
        cols(i["mix_norm"][0]), cols(i["ffn_norm"][0]), cols(i["mix_norm"][1]), cols(i["ffn_norm"][1]),
        cols(i["norm_ffn1_2"][0]), cols(i["norm_mix_2"][0]), cols(i["norm_ffn2_2"][0]), cols(i["hy_gla_norm"][0]),
        twice(i["hy_sb_q_norm"][0]), twice(i["hy_sb_k_norm"][0]), cols(i["cv_b_dw"][0]), cols(i["cv_ln_g"][0]),
        cols(i["cv_ln_b"][0]), cols(i["pool_scale_2"][0]),
        i["cv_w_dw"][0].reshape(31, 8, 128).transpose(2, 1, 0).reshape(128, 248)], axis=1)

    def rows(x):
        return np.broadcast_to(x.reshape(1, -1), (128, x.size))

    return {
        "x": i["x"].reshape(2, 128, 1024), "w": np.stack(seq),
        "wg": col["glr"].reshape(8, 128, 16).transpose(1, 0, 2).reshape(128, 128), "wg2": i["hy_w_gate2"][0],
        "cst": cst, "par": par, "b_gate": rows(i["hy_b_gate"][0]),
        "b_pw1": rows(i["cv_b_pw1"][0].reshape(2, 4, 256).transpose(1, 0, 2)),
        "b_pw2": rows(i["cv_b_pw2"][0]), "gate_bias": rows(i["gate_bias_2"][0]),
        "norm_final": rows(i["norm_final_2"]), "cosin": cosin, "rmask": rmask, "pmat": pmat,
    }


def kernel(**inputs):
    import numpy as np
    import concourse.bacc as bacc
    from concourse.bass_utils import run_bass_kernel_spmd
    laid = layout({k: np.asarray(v) for k, v in inputs.items()})
    nc = bacc.Bacc("TRN2", target_bir_lowering=False, num_devices=1)
    arrays, aps = {}, {}
    for name, a in laid.items():
        a = np.ascontiguousarray(a)
        arrays["in_" + name] = a
        aps[name] = nc.dram_tensor("in_" + name, a.shape, mybir.dt.from_np(a.dtype), kind="ExternalInput").ap()
    out = nc.dram_tensor("out_0", (2, 128, 1024), F32, kind="ExternalOutput").ap()
    build(nc, aps["x"], aps["w"], aps["wg"], aps["wg2"], aps["cst"], aps["par"],
          {n: aps[n] for n in ("b_gate", "b_pw1", "b_pw2", "gate_bias", "norm_final")}, aps["cosin"], aps["rmask"],
          aps["pmat"], out)
    r = run_bass_kernel_spmd(nc, [arrays], core_ids=[0])
    return r.results[0]["out_0"].reshape(1, 256, 1024)
```

```python
from contextlib import ExitStack

import concourse.bass as bass
from concourse import mybir

P = 128
D = 1024
T = 256
FC = 11
UC = 2048
R = 4
S = 4

F32 = mybir.dt.float32
F32R = mybir.dt.float32r
ALU = mybir.AluOpType
ACT = mybir.ActivationFunctionType
AXX = mybir.AxisListType.X

EPS = 1e-6
NK = {"ident": 0, "later": 128, "ones": 256, "mask": 384, "rest": 640, "blk": 768}
NKW = 770
PAR = {"mix0": 0, "ffn0": 8, "mix1": 16, "ffn1": 24, "n1": 32, "nm": 40, "n2": 48, "gla": 56, "gq": 57, "gk": 58,
       "b_dw": 59, "ln_g": 67, "ln_b": 75, "pool": 83, "w_dw": 91}
PARW = 91 + 8 * 31
UNITS = {"sq": 2, "sk": 2, "sv": 2, "gqk": 2, "gv": 2, "gr": 2, "hout": 4, "ff0": 33, "pw1": 8, "pw2": 4, "ff1": 33,
         "ffa": 33, "p": 4, "pw": 1, "gp": 8, "q": 4, "k": 4, "v": 4, "gret": 4, "gu": 8, "out2": 4, "ffb": 33}


def build(nc, xin, wst, wg, wg2, cst, par, brow, cosin, rmask, pmat, out):
    NU = wst.shape[0]
    assert NU == sum(UNITS.values())
    with ExitStack() as ctx:
        def sb(name, shape, dt=F32):
            return ctx.enter_context(nc.sbuf_tensor(name, shape, dt))

        class Engine:

            def __init__(self, name):
                self.name, self.items, self.count, self.seen = name, [], 0, {}
                self.sem = ctx.enter_context(nc.semaphore("done_" + name))

            def wait(self, *tokens):
                for tok in tokens:
                    if tok is None:
                        continue
                    if isinstance(tok, list):
                        self.wait(*tok)
                        continue
                    sem, value = tok
                    if self.seen.get(sem.name, 0) < value:
                        self.seen[sem.name] = value
                        self.items.append(lambda e, sem=sem, value=value: e.wait_ge(sem, value))

            def do(self, fn, *tokens, inc=True):
                self.wait(*tokens)
                if not inc:
                    self.items.append(fn)
                    return None
                self.count += 1
                self.items.append(lambda e: fn(e).then_inc(self.sem, 1))
                return self.sem, self.count

        pe, act, dve, pool, sp = Engine("pe"), Engine("act"), Engine("dve"), Engine("pool"), Engine("sp")

        raw = sb("raw", [P, R, UC])
        whi = sb("whi", [P, S, UC], F32R)
        wlo = sb("wlo", [P, S, UC], F32R)
        xh = sb("xh", [P, 8, T], F32R)
        xl = sb("xl", [P, 8, T], F32R)
        yh = sb("yh", [P, 8, T], F32R)
        yl = sb("yl", [P, 8, T], F32R)
        h = sb("h", [P, 2, D])
        kc = sb("kc", [P, NKW])
        pr = sb("pr", [P, PARW])
        st = sb("st", [P, 96])
        sil = sb("sil", [P, 2, T])
        hid = sb("hid", [P, 2, T])
        AR = sb("AR", [P, 14080])
        ps = [ctx.enter_context(nc.psum_tensor(f"ps{i}", [P, 512], F32)) for i in range(8)]
        free = [None] * 8

        def const(name, n=P):
            return kc[:, NK[name]:NK[name] + n]

        def parm(name, k=0, n=1):
            return pr[:, PAR[name] + k:PAR[name] + k + n]

        ident = const("ident")

        slot_sem = [ctx.enter_context(nc.semaphore(f"raw{i}")) for i in range(R)]

        def load(dst, src, *tokens):
            sem = ctx.enter_context(nc.semaphore(f"load{len(sp.items)}"))
            sp.wait(*tokens)
            sp.items.append(lambda e: e.dma_start(dst, src).then_inc(sem, 16))
            return sem, 16

        hi_done, lo_done, unit_done, piece_done = {}, {}, {}, {}
        loaded = [0]
        split = [0]

        def load_unit():
            v = loaded[0]
            if v < NU and (v < R or v - R in lo_done):
                sp.wait(lo_done.get(v - R))
                sem = slot_sem[v % R]
                sp.items.append(lambda e: e.dma_start(raw[:, v % R, :], wst[v]).then_inc(sem, 16))
                loaded[0] += 1
                return True
            return False

        def pump(most=S):
            while True:
                while load_unit():
                    pass
                most -= 1
                v = split[0]
                if most < 0 or v >= NU or v >= loaded[0] or not (v < S or v - S in unit_done):
                    return
                split[0] += 1
                arrived = (slot_sem[v % R], 16 * (v // R + (0 if v % R < 2 else 1)))
                hi_done[v] = act.do(lambda e, v=v: e.copy(whi[:, v % S, :], raw[:, v % R, :]),
                                    arrived, unit_done.get(v - S))
                lo_done[v] = (pool if v in on_pool else dve).do(lambda e, v=v: e.tensor_tensor(wlo[:, v % S, :], raw[:, v % R, :],
                                                                   whi[:, v % S, :].bitcast(F32), ALU.subtract),
                                    hi_done[v], unit_done.get(v - S))

        first = UNITS["sq"] + UNITS["sk"] + UNITS["sv"] + UNITS["gqk"] + UNITS["gv"] + UNITS["gr"] + UNITS["hout"]
        first += UNITS["ff0"]
        on_pool = (first + 3, first + 5, first + 7, first + 9, first + 11)

        at = [0]
        plan, here = {}, [0]

        def later(n, fn):
            plan.setdefault(here[0] + n, []).append(fn)

        def gap():
            for fn in plan.pop(here[0], []):
                fn()
            here[0] += 1

        def gaps_left():
            while plan:
                gap()

        def take(n, ahead=S):
            pump(ahead)
            us = list(range(at[0], at[0] + n))
            at[0] += n
            for u in us:
                assert u in lo_done
            return us

        def mm3(o, ah, al, bh, bl, start, stop, skip=False, inc=False):
            pe.do(lambda e: e.matmul(o, ah, bh, start=start, stop=False, skip_group_check=skip), inc=False)
            pe.do(lambda e: e.matmul(o, ah, bl, start=False, stop=False, skip_group_check=skip), inc=False)
            return pe.do(lambda e: e.matmul(o, al, bh, start=False, stop=stop, skip_group_check=skip), inc=inc)

        def mm(o, a, b, start=True, stop=True, skip=False, inc=True, deps=()):
            return pe.do(lambda e: e.matmul(o, a, b, start=start, stop=stop, skip_group_check=skip), *deps, inc=inc)

        def tr(o, i, deps=(), inc=True):
            return pe.do(lambda e: e.transpose(o, i, ident[0:i.shape[0], 0:i.shape[0]]), *deps, inc=inc)

        def A(out_, in_, func, *deps, scale=1.0, bias=0.0, accum=None):
            return act.do(lambda e: e.activation(out_, in_, func, bias=bias, scale=scale, accum_out=accum)
                          if accum is not None else e.activation(out_, in_, func, bias=bias, scale=scale), *deps)

        def tables(name):
            act.do(lambda e: e.preload_act_table_set(name), inc=False)

        def TT(out_, a, b, op, *deps, eng=dve):
            return eng.do(lambda e: e.tensor_tensor(out_, a, b, op), *deps)

        def TS(out_, a, s1, s2, op0, op1, *deps, eng=dve):
            if op1 is None:
                return eng.do(lambda e: e.tensor_scalar(out_, a, s1, None, op0), *deps)
            return eng.do(lambda e: e.tensor_scalar(out_, a, s1, s2, op0, op1), *deps)

        def STT(out_, a, s, b, op0, op1, *deps):
            return dve.do(lambda e: e.scalar_tensor_tensor(out=out_, in0=a, scalar=s, in1=b, op0=op0, op1=op1), *deps)

        def rsqrt(out_, ss, n, *deps):
            a = TS(out_, ss, 1.0 / n, EPS, ALU.mult, ALU.add, *deps)
            return TT(out_, out_, nhalf[:, 0:out_.shape[1]], ALU.pow, a, nhalf_t, eng=pool)

        flip = [0]

        def tbank():
            flip[0] ^= 1
            return 6 + flip[0]

        def xpose_half(src, t, half, dh, dl, gain, ready, *freed):
            b = tbank()
            cols = slice(P * t, P * t + P)
            ks = range(4 * half, 4 * half + 4)
            for i, k in enumerate(ks):
                tok = tr(ps[b][:, 128 * i:128 * i + 128], src[:, 128 * k:128 * k + 128], (ready, free[b]), inc=i == 3)
            if all(gain(k) is None for k in ks):
                src4 = ps[b][:, :].rearrange("p (k c) -> p k c", k=4)
                hi4, lo4 = (x[:, 4 * half:4 * half + 4, cols] for x in (dh, dl))
                a = A(hi4, src4, ACT.Copy, tok, *freed)
                d = TT(lo4, src4, hi4.bitcast(F32), ALU.subtract, a)
            else:
                for i, k in enumerate(ks):
                    a = A(dh[:, k, cols], ps[b][:, 128 * i:128 * i + 128], ACT.Copy, tok, *freed, scale=gain(k))
                for i, k in enumerate(ks):
                    d = STT(dl[:, k, cols], ps[b][:, 128 * i:128 * i + 128], gain(k),
                            dh[:, k, cols].bitcast(F32), ALU.mult, ALU.subtract, a)
            free[b] = d
            return d

        def xpose(src, t, dh, dl, gain, ready, *freed):
            return [xpose_half(src, t, half, dh, dl, gain, ready[half], *freed) for half in range(2)]

        nhalf = sb("nhalf", [P, 16])
        sts = [sb(f"state{n}", [P, 2, 256]) for n in range(2)]
        rb, dgr = sts[0][:, 0, :], sts[1][:, 0, :]
        zer = [pool.do(lambda e, n=n: e.memset(sts[n][:, :, :], 0.0)) for n in range(2)]
        nhalf_t = pool.do(lambda e: e.memset(nhalf[:, :], -0.5))
        rstd = st[:, 0:2]
        ss = st[:, 2:4]
        x_ready = [[None, None], [None, None]]
        x_used = [None]
        y_used = [None]
        h_ready = [[None, None], [None, None]]
        rstd_ready = [None, None]
        rstd_used = [None, None]
        junk = AR[:, 13056:14080]
        junk_used = [None]

        def norm(t, name):
            x_ready[t] = xpose(h[:, t, :], t, xh, xl, lambda k: parm(name, k), h_ready[t], x_used[0])
            a = A(junk, h[:, t, :], ACT.Square, *h_ready[t], junk_used[0], accum=ss[:, t:t + 1])
            junk_used[0] = a
            rstd_ready[t] = rsqrt(rstd[:, t:t + 1], ss[:, t:t + 1], D, a, rstd_used[t])

        def in_chunk(evac, second=None, banks=(4, 5), lhs=None):
            us = take(2, min(1, at[0]) if second else S)
            lh, ll, ready = lhs or (xh, xl, x_ready)
            for t in range(2):
                b = banks[t]
                pe.wait(free[b])
                for j, u in enumerate(us):
                    pe.wait(ready[t][j])
                    for k in range(4):
                        kk = 4 * j + k
                        pe.wait(piece_done.get((u, k), lo_done[u]))
                        tok = mm3(ps[b][:, :], lh[:, kk, P * t:P * t + P], ll[:, kk, P * t:P * t + P],
                                  whi[:, u % S, 512 * k:512 * k + 512], wlo[:, u % S, 512 * k:512 * k + 512],
                                  kk == 0, kk == 7, inc=k == 3)
                    if t == 1:
                        unit_done[u] = tok
                    if j == 1:
                        evac(t, b, tok)
                    if second and t == 0 and j == 0:
                        second()
                        pump()
                    gap()
                    if t == 1 and j == 0:
                        pump()
            return tok

        acc = [(0, 1), (2, 3)]

        def out_part(u, t, k0, lh, ll, ready, first, last):
            pe.wait(lo_done[u], ready[t])
            if first:
                pe.wait(*[free[b] for b in acc[t]])
            for k in range(2):
                lhs = [x[:, k0 + k, P * t:P * t + P] for x in (lh, ll)]
                for half in range(2):
                    c = 1024 * k + 512 * half
                    tok = mm3(ps[acc[t][half]][:, :], lhs[0], lhs[1], whi[:, u % S, c:c + 512],
                              wlo[:, u % S, c:c + 512], first and k == 0, last and k == 1,
                              inc=k == 1 and half == 1)
            if t == 1:
                unit_done[u] = tok
            return tok

        def out_unit(k0, lh, ll, ready, first):
            u, = take(1)
            for t in range(2):
                tok = out_part(u, t, k0, lh, ll, ready, first, False)
            return tok

        def out_last(k0s, lh, ll, readies, scale, following):
            us = take(2)
            for n in range(2):
                tok = out_part(us[n], 0, k0s[n], lh, ll, readies[n], False, n == 1)
            residual(0, tok, scale)
            out_part(us[0], 1, k0s[0], lh, ll, readies[0], False, False)
            if following:
                norm(0, following)
            tok = out_part(us[1], 1, k0s[1], lh, ll, readies[1], False, True)
            residual(1, tok, scale)
            return tok

        def residual(t, tok, scale=None):
            for half in range(2):
                cols = slice(512 * half, 512 * half + 512)
                b = acc[t][half]
                if scale is None:
                    d = TT(h[:, t, cols], ps[b][:, :], h[:, t, cols], ALU.add, tok, h_ready[t][half])
                else:
                    d = STT(h[:, t, cols], ps[b][:, :], scale[0][t], h[:, t, cols], ALU.mult, ALU.add, tok,
                            h_ready[t][half], scale[1])
                    rstd_used[t] = d
                h_ready[t][half] = free[b] = d

        def square_out(lh, ll, ready, following, ks=(0, 2, 4, 6)):
            def r(k):
                return [ready[t][k * len(ready[t]) // 8] for t in range(2)]
            for n in range(2):
                out_unit(ks[n], lh, ll, r(ks[n]), n == 0)
            return out_last(ks[2:], lh, ll, (r(ks[2]), r(ks[3])), None, following)

        def turned_chunk(gates, ups):
            us = take(2)
            for j, u in enumerate(us):
                pe.wait(lo_done[u])
                for half, b in enumerate((4, 5)):
                    if j == 0:
                        pe.wait(free[b])
                    for m in range(2):
                        for k in range(4):
                            c = 512 * k + 256 * half + P * m
                            tok = mm3(ps[b][:, 256 * m:256 * m + 256], whi[:, u % S, c:c + P],
                                      wlo[:, u % S, c:c + P], xh[:, 4 * j + k, :], xl[:, 4 * j + k, :],
                                      j == 0 and k == 0 and m == 0, j == 1 and k == 3, skip=True,
                                      inc=m == 1 and k == 3)
                    if j == 1:
                        (gates, ups)[half](b, tok)
                    if half == 1:
                        unit_done[u] = tok
                    gap()
                if j == 0:
                    pump()
            return tok

        def ffn(name, weight, following):
            ht_ready = {}
            down_done = {}
            hid_done = [None, None]
            last = {"sil": None, "hid": None}

            def first_evac(t, b, tok):
                a = A(sil[:, t, :], ps[b][:, 0:256], ACT.Silu, tok, rstd_ready[t], scale=rstd[:, t:t + 1])
                free[b] = hid_done[t] = TT(hid[:, t, :], ps[b][:, 256:512], sil[:, t, :], ALU.mult, a)

            def first_turn():
                b = tbank()
                for t in range(2):
                    for k in range(2):
                        tok = tr(ps[b][:, 256 * k + P * t:256 * k + P * t + P], hid[:, t, P * k:P * k + P],
                                 (hid_done[t], free[b]), inc=k == 1)
                last["hid"] = tok
                src = ps[b][:, :].rearrange("p (k c) -> p k c", k=2)
                a = A(yh[:, 0:2, :], src, ACT.Copy, tok, y_used[0])
                free[b] = ht_ready[0] = TT(yl[:, 0:2, :], src, yh[:, 0:2, :].bitcast(F32), ALU.subtract, a)

            rb_t = {}

            def diagonal():
                for t in range(2):
                    rb_t[t] = TS(dgr[:, P * t:P * t + P], ident, rstd[:, t:t + 1], 1.0, ALU.mult, ALU.mult,
                                 rstd_ready[t])

            def spread():
                b = tbank()
                tok = mm(ps[b][:, 0:T], const("ones"), dgr, deps=(rb_t[0], rb_t[1], free[b]))
                free[b] = rb_t["done"] = A(rb, ps[b][:, 0:T], ACT.Copy, tok)

            def gates(b, tok):
                v = ps[b][:, :].rearrange("p (k c) -> p k c", k=2)
                d = TT(sil[:, :, :], v, rb.unsqueeze(1).to_broadcast([P, 2, T]), ALU.mult, tok, rb_t["done"])
                free[b] = d
                last["sil"] = A(sil[:, :, :], sil[:, :, :], ACT.Silu, d)

            def ups(j):
                def f(b, tok):
                    v = ps[b][:, :].rearrange("p (k c) -> p k c", k=2)
                    d = free[b] = TT(hid[:, :, :], v, sil[:, :, :], ALU.mult, tok, last["sil"], last["hid"])
                    k0 = 2 * (j % 4)
                    a = A(yh[:, k0:k0 + 2, :], hid[:, :, :], ACT.Copy, d, down_done.get(j - 4), y_used[0])
                    ht_ready[j] = TT(yl[:, k0:k0 + 2, :], hid[:, :, :], yh[:, k0:k0 + 2, :].bitcast(F32),
                                     ALU.subtract, a)
                return f

            def down(j):
                down_done[j] = out_unit(2 * (j % 4), yh, yl, [ht_ready[j]] * 2, j == 0)

            later(3, diagonal)
            later(5, spread)
            in_chunk(first_evac, second=lambda: norm(1, name))
            later(0, first_turn)
            for j in range(1, FC):
                x_tok = turned_chunk(gates, ups(j))
                if j < FC - 2:
                    down(j - 1)
            x_used[0] = x_tok
            down(FC - 3)
            scale = []
            for t in range(2):
                if weight == 1.0:
                    scale.append(rstd[:, t:t + 1])
                else:
                    scale.append(st[:, 92 + t:93 + t])
                    TS(scale[t], rstd[:, t:t + 1], weight, None, ALU.mult, None, rstd_ready[t])
            scale_t = dve.sem, dve.count
            j = FC - 2
            y_used[0] = out_last([2 * (i % 4) for i in (j, j + 1)], yh, yl, [[ht_ready[i]] * 2 for i in (j, j + 1)],
                                 (scale, scale_t), following)

        def ar(start, *shape):
            n = 1
            for s in shape:
                n *= s
            v = AR[:, start:start + n]
            names = "abcd"[:len(shape)]
            if len(shape) > 1:
                v = v.rearrange(f"p ({' '.join(names)}) -> p {' '.join(names)}",
                                **{c: s for c, s in zip(names, shape)})
            return v

        h_ready[0][0] = load(h[:, 0, 0:512], xin[0][:, 0:512])
        tok_i = load(ident, cst[:, 0:P])
        h_ready[0][1] = load(h[:, 0, 512:1024], xin[0][:, 512:1024])
        tok_p = load(pr[:, :], par)
        raw_piece = {}
        for v, n in ((0, 4), (1, 2)):
            for k in range(n):
                cols = slice(UC // n * k, UC // n * (k + 1))
                raw_piece[v, k] = load(raw[:, v, cols], wst[v][:, cols])
            loaded[0] += 1
        tok = load(h[:, 1, :], xin[1])
        h_ready[1] = [tok, tok]
        wgr = ar(0, 128)
        wg2s = AR[0:16, 128:384]
        bg = ar(384, 256)
        tok_wg = load(wgr, wg)
        tok_k = load(kc[:, P:NKW], cst[:, P:NKW])
        while load_unit():
            pass
        tok_wg2 = load(wg2s, wg2)
        tok_bg = load(bg, brow["b_gate"])
        act.do(lambda e: e.preload_act_table_set("natural_log_exp_and_others"), inc=False)
        pe.wait(tok_i)
        dve.wait(tok_p)
        act.wait(tok_p)

        gqn = ar(640, 2, 512)
        gvn = ar(1664, 2, 512)
        srn = ar(2688, 2, 512)
        svn = ar(3712, 2, 512)
        sqn = ar(4736, 2, 512)
        sqT = ar(5760, 4, T)
        skT = ar(6784, 4, T)
        tmp = ar(7808, 2, 512)
        mixn = ar(8832, 2, D)
        gqT = ar(10880, 2, T)
        la = ar(11392, 2, T)
        zt = ar(11904, 3, 384)
        two = sb("two", [P, 2, 286], F32R)
        wgh, wgl = two[:, 0, 0:256], two[:, 1, 0:256]
        gq8 = st[:, 4:5]

        read = {}

        def heads_evac(dst, gain, gain_tok, key, tmp):
            def f(t, b, tok):
                a = A(sqn[:, t, :], ps[b][:, :], ACT.Copy, tok, rstd_ready[t], read.get(("sqn", t)),
                      scale=rstd[:, t:t + 1])
                free[b] = a
                q3 = sqn[:, t, :].rearrange("p (h d) -> p h d", h=8)
                t3 = tmp[:, t, :].rearrange("p (h d) -> p h d", h=8)
                s8 = st[:, 8 + 8 * t:16 + 8 * t]
                d = TT(tmp[:, t, :], sqn[:, t, :], sqn[:, t, :], ALU.mult, a)
                d = dve.do(lambda e: e.tensor_reduce(s8, t3, AXX, ALU.add), d)
                d = rsqrt(s8, s8, 64, d)
                d = TT(t3, q3, s8.unsqueeze(2).to_broadcast([P, 8, 64]), ALU.mult, d, eng=pool)
                read[("sqn", t)] = d

                def turned():
                    b2 = tbank()
                    for i in range(4):
                        tk = tr(ps[b2][:, P * i:P * i + P], tmp[:, t, P * i:P * i + P], (d, free[b2]), inc=i == 3)
                    read[("tmp", t)] = tk
                    free[b2] = key[t] = A(dst[:, :, P * t:P * t + P],
                                          ps[b2][:, :].rearrange("p (k c) -> p k c", k=4), ACT.Copy, tk, gain_tok,
                                          scale=gain)
                later(4 if t == 0 else 3, turned)
            return f

        def plain(dst, key, func=ACT.Copy):
            def f(t, b, tok):
                free[b] = key[t] = A(dst[:, t, :], ps[b][:, :], func, tok, rstd_ready[t], scale=rstd[:, t:t + 1])
            return f

        sq_t, sk_t, sv_t, gqk_t, gv_t, gr_t = ([None, None] for _ in range(6))

        def piece(v, n, k):
            cols = slice(UC // n * k, UC // n * (k + 1))
            a = act.do(lambda e: e.copy(whi[:, v, cols], raw[:, v, cols]), raw_piece[v, k])
            d = TT(wlo[:, v, cols], raw[:, v, cols], whi[:, v, cols].bitcast(F32), ALU.subtract, a)
            for q in range(4 // n * k, 4 // n * (k + 1)):
                piece_done[v, q] = d
            hi_done[v], lo_done[v] = a, d

        for half in range(2):
            x_ready[0][half] = xpose_half(h[:, 0, :], 0, half, xh, xl, lambda k: parm("mix0", k), h_ready[0][half])
            piece(0, 4, 2 * half)
            piece(0, 4, 2 * half + 1)
        a = junk_used[0] = A(junk, h[:, 0, :], ACT.Square, *h_ready[0], accum=ss[:, 0:1])
        rstd_ready[0] = rsqrt(rstd[:, 0:1], ss[:, 0:1], D, a)
        piece(1, 2, 0)
        piece(1, 2, 1)
        split[0] = 2
        gq8_t = TS(gq8, parm("gq"), 0.125, None, ALU.mult, None)
        in_chunk(heads_evac(sqT, gq8, gq8_t, sq_t, mixn[:, :, 0:512]), second=lambda: norm(1, "mix0"))
        g_a = act.do(lambda e: e.copy(wgh[:, 0:128], wgr), tok_wg)
        g_d = TT(wgl[:, 0:128], wgr, wgh[:, 0:128].bitcast(F32), ALU.subtract, g_a)
        g_z = [act.do(lambda e, w=w: e.copy(w[:, 128:256], wgr), tok_wg) for w in (wgh, wgl)]
        for engine in (pe, act, dve, pool):
            engine.wait(tok_k)
        in_chunk(heads_evac(skT, parm("gk"), None, sk_t, tmp))

        glT = AR[0:16, 13088:13344]
        la2 = la.rearrange("p a b -> p (a b)")
        e1 = ar(7808, 512)
        gl = {}

        def gate_rank():
            b = tbank()
            pe.wait(free[b], g_d, g_z)
            for k in range(8):
                tok = mm3(ps[b][:, 0:256], wgh[:, 16 * k:16 * k + P], wgl[:, 16 * k:16 * k + P], xh[:, k, :],
                          xl[:, k, :], k == 0, k == 7, inc=k == 7)
            free[b] = gl["glT"] = A(glT, ps[b][0:16, 0:256], ACT.Copy, tok, junk_used[0])

        def gate_log():
            b = tbank()
            pe.wait(gl["glT"], tok_wg2, free[b])
            for t in range(2):
                tok = mm(ps[b][:, 256 * t:256 * t + 256], glT[:, P * t:P * t + P], wg2s, inc=t == 1)
            for t in range(2):
                d = STT(la[:, t, :], ps[b][:, 256 * t:256 * t + 256], rstd[:, t:t + 1], bg, ALU.mult, ALU.add, tok,
                        tok_bg, rstd_ready[t])
            free[b] = d
            a = A(e1, la2, ACT.Abs, d, *[read[("tmp", t)] for t in range(2)])
            a = A(e1, e1, ACT.Exp, a, scale=-1.0)
            a = A(e1, e1, ACT.Ln, a, bias=1.0)
            gl["la"] = STT(la2, la2, 0.0, e1, ALU.min, ALU.subtract, a)

        def decays():
            b = tbank()
            pe.wait(free[b], gl["la"])
            for t in range(2):
                tok = mm(ps[b][:, 256 * t:256 * t + 256], const("rest"), la[:, t, :], inc=t == 1)
            gl["e"] = free[b] = A(e1, ps[b][:, :], ACT.Exp, tok, gl["la"], scale=1.0 / 16)
            b = tbank()
            pe.wait(free[b])
            for j in range(2):
                for t in range(2):
                    c = 4 * j + 2 * t
                    tok = mm(ps[b][:, c:c + 2], la[:, t, P * j:P * j + P], const("blk", 2), inc=j == 1 and t == 1)
            gl["dec"] = free[b] = A(st[:, 24:32], ps[b][:, 0:8], ACT.Exp, tok, scale=1.0 / 16)

        mask2 = const("mask", 256).rearrange("p (a c) -> p a c", a=2)
        bufs = [(zt[:, 0, :], zt[:, 1, :], zt[:, 2, :]),
                (ar(4736, 384), ar(5120, 384), ar(13344, 384))]
        zr = {}

        def z_scores(i):
            pr0, j = 64 * (i % 2), i // 2
            kT, qT = skT[pr0:pr0 + 64, j, :], sqT[pr0:pr0 + 64, j, :]
            z = ps[0]
            pe.wait(free[0], *sq_t, *sk_t)
            mm(z[:, 0:256], kT[:, 0:128], qT[:, 0:256], inc=False)
            tok = mm(z[:, 256:384], kT[:, 128:256], qT[:, 128:256])
            ls, kp, w = bufs[i % 2]
            a = A(w, z[:, 0:384], ACT.Abs, tok, zr.get(("w", i - 2)), *[read[("sqn", t)] for t in range(2)])
            a = A(w, w, ACT.Exp, a, scale=-1.0)
            a = A(w, w, ACT.Ln, a, bias=1.0)
            d = STT(ls, z[:, 0:384], 0.0, w, ALU.min, ALU.subtract, a, zr.get(("ls", i - 2)))
            d = TT(kp, ls, z[:, 0:384], ALU.subtract, d, zr.get(("kp", i - 2)))
            free[0] = d
            kd = kp.rearrange("p (a c) -> p a c", a=3)[:, 0:3:2, :]
            zr[("keep", i)] = TT(kd, kd, mask2, ALU.mult, d)

        def z_between(i):
            ls, kp, w = bufs[i % 2]
            bt = ps[1]
            pe.wait(free[1], zr[("keep", i)])
            mm(bt[:, 0:256], const("later"), kp[:, 0:256], start=True, stop=False, skip=True, inc=False)
            mm(bt[:, 128:256], const("ones"), kp[:, 256:384], start=False, stop=False, skip=True, inc=False)
            tok = mm(bt[:, 256:384], const("later"), kp[:, 256:384], start=False, stop=True, skip=True)
            zr[("kp", i)] = tok
            d = TT(w, ls, bt[:, 0:384], ALU.add, tok)
            free[1] = zr[("ls", i)] = d
            a = A(w, w, ACT.Exp, d)
            wd = w.rearrange("p (a c) -> p a c", a=3)[:, 0:3:2, :]
            zr[("weights", i)] = TT(wd, wd, mask2, ALU.mult, a)

        sb_ready = {}

        def z_values(i):
            ls, kp, w = bufs[i % 2]
            bk, c0, rows = 2 + i // 4, 256 * (i // 2 % 2), slice(64 * (i % 2), 64 * (i % 2) + 64)
            pe.wait(free[bk], zr[("weights", i)], *sv_t)
            hc = slice(64 * i, 64 * i + 64)
            mm(ps[bk][rows, c0:c0 + 256], svn[:, 0, hc], w[:, 0:256], start=True, stop=False, skip=True, inc=False)
            tok = zr[("w", i)] = mm(ps[bk][rows, c0 + 128:c0 + 256], svn[:, 1, hc], w[:, 256:384], start=False,
                                    stop=True, skip=True)
            if i % 4 == 3:
                src = ps[bk][:, :].rearrange("p (k c) -> p k c", k=2)
                ks = slice(4 + i // 4 * 2, 6 + i // 4 * 2)
                a = A(yh[:, ks, :], src, ACT.Copy, tok)
                free[bk] = sb_ready[i // 4] = TT(yl[:, ks, :], src, yh[:, ks, :].bitcast(F32), ALU.subtract, a)

        def turn_q():
            b = tbank()
            for j in range(2):
                for t in range(2):
                    c = 256 * j + P * t
                    tok = tr(ps[b][:, c:c + P], gqn[:, t, P * j:P * j + P], (gqk_t[t], free[b]),
                             inc=j == 1 and t == 1)
            gl["q"] = free[b] = A(gqT, ps[b][:, :].rearrange("p (j c) -> p j c", j=2), ACT.Copy, tok, scale=0.125)

        def keys():
            e3 = e1.rearrange("p (t c) -> p t c", t=2)
            gl["k"] = TT(gqn[:, :, 256:512], gqn[:, :, 256:512], e3, ALU.mult, gl["e"], *gqk_t)

        o_done, s_done, g_done = {}, {}, {}

        def state(n):
            t, c = divmod(n, 2)
            rows = slice(64 * c, 64 * c + 64)
            ub = tbank()
            pe.wait(free[ub], gl["k"], gv_t[t])
            for j in range(2):
                tok = mm(ps[ub][:, 256 * j:256 * j + 256], gqn[rows, t, 256 + P * j:256 + P * j + P],
                         gvn[rows, t, 256 * j:256 * j + 256], inc=j == 1)
            cur, prev = sts[n % 2], sts[(n + 1) % 2]
            for g in range(2):
                rr, cc = slice(64 * g, 64 * g + 64), slice(P * g, P * g + P)
                for j in range(2):
                    uu = ps[ub][rr, 256 * j + P * g:256 * j + P * g + P]
                    if n == 0:
                        d = dve.do(lambda e, o=cur[rr, j, cc], i=uu: e.tensor_copy(o, i), tok, *zer)
                    else:
                        d = STT(cur[rr, j, cc], prev[rr, j, cc], st[rr, 24 + 4 * j + n:25 + 4 * j + n], uu,
                                ALU.mult, ALU.add, tok, gl["dec"], o_done.get(n - 2), s_done.get(n - 1))
            s_done[n] = free[ub] = d

        def queried(n):
            t, c = divmod(n, 2)
            rows = slice(64 * c, 64 * c + 64)
            ob = tbank()
            pe.wait(s_done[n], gl["q"], free[ob])
            for j in range(2):
                o_done[n] = mm(ps[ob][rows, 256 * j:256 * j + 256], gqT[:, j, 64 * n:64 * n + 64],
                               sts[n % 2][:, j, :], inc=j == 1)
            g_done[n] = free[ob] = A(mixn[rows, t, 0:512], ps[ob][rows, :], ACT.Copy, o_done[n])

        gla_out = [None, None]

        def gla_norm(t):
            m = mixn[:, t, 0:512]
            m3 = m.rearrange("p (h d) -> p h d", h=4)
            tp = tmp[:, t, :]
            tp3 = tp.rearrange("p (h d) -> p h d", h=4)
            s4 = st[:, 32 + 4 * t:36 + 4 * t]
            d = TT(tp, m, m, ALU.mult, g_done[2 * t], g_done[2 * t + 1], gl["k"])
            d = dve.do(lambda e: e.tensor_reduce(s4, tp3, AXX, ALU.add), d)
            d = rsqrt(s4, s4, 128, d)
            gla_out[t] = TT(m3, m3, s4.unsqueeze(2).to_broadcast([P, 4, 128]), ALU.mult, d)

        steps = [[] for _ in range(22)]
        first = [2, 3, 5, 7, 8, 10, 12, 13]
        for i in range(8):
            steps[first[i] + 3].append(lambda i=i: z_values(i))
        for i in range(8):
            steps[first[i] + 2].append(lambda i=i: z_between(i))
        for i in range(8):
            steps[first[i]].append(lambda i=i: z_scores(i))
        steps[1].append(gate_rank)
        steps[4].append(gate_log)
        steps[6].append(decays)
        steps[8].append(turn_q)
        steps[9].append(keys)
        for n, (s0, s1) in enumerate(((10, 11), (11, 13), (13, 14), (14, 15))):
            steps[s0].append(lambda n=n: state(n))
            steps[s1].append(lambda n=n: queried(n))
        steps[14].append(lambda: gla_norm(0))
        for n, fns in enumerate(steps):
            for fn in fns:
                later(n, fn)
        in_chunk(plain(svn, sv_t))
        in_chunk(plain(gqn, gqk_t))
        in_chunk(plain(gvn, gv_t))
        x_used[0] = in_chunk(plain(srn, gr_t))

        acc[0], acc[1] = (4, 5), (2, 0)
        gla_norm(1)
        tables("silu_and_others")
        u, = take(1, 0)
        for t in range(2):
            out_part(u, t, 4, yh, yl, [sb_ready[0]] * 2, True, False)
            gap()
        assert not plan
        y_ready = [None, None]
        for t in range(2):
            gr_t[t] = A(srn[:, t, :], srn[:, t, :], ACT.Silu, gr_t[t])
            m = mixn[:, t, 0:512]
            gla_out[t] = TT(m, m, srn[:, t, :], ALU.mult, gla_out[t], gr_t[t])
        u, = take(1)
        for t in range(2):
            out_part(u, t, 6, yh, yl, [sb_ready[1]] * 2, False, False)
            y_ready[t] = xpose_half(mixn[:, t, :], t, 0, yh, yl, lambda k: parm("gla"), gla_out[t], y_used[0])
        y_used[0] = out_last((0, 2), yh, yl, [y_ready] * 2, None, "ffn0")
        acc[0], acc[1] = (0, 1), (2, 3)

        arena_free = [y_used[0], list(free)]
        ffn("ffn0", 1.0, "mix1")

        MT, KT = (3, 4, 5, 6), 29
        ND, NP_ = MT[0], len(MT)
        mtaps = [(c, w) for c in range(NP_) for w in range(KT if c == 0 else 31)]
        bp1 = ar(0, 2048)
        bp2 = ar(2048, 1024)
        t_bp1 = load(bp1, brow["b_pw1"], *arena_free)
        t_bp2 = load(bp2, brow["b_pw2"])
        glu = ar(3072, 2, 512)
        upad = ar(4096, 8, 286)
        cv = ar(6384, 8, T)
        sq = ar(8432, 8, T)
        mu = ar(10480, T)
        dg = ar(10736, 2, P)
        u2 = ar(10992, 2, 2, 256)
        wlow = ar(12016, 31 * NP_)
        wdh = sb("wdh", [P, 31 * NP_], F32R)
        z0 = pool.do(lambda e: e.memset(upad[:, :, 0:30], 0.0), *arena_free)
        gl_read, gl_done, up_t = {}, {}, [None] * 8
        cvt = [None] * 8

        wd_a = act.do(lambda e: e.copy(wdh[:, :], parm("w_dw", 31 * ND, 31 * NP_)))
        wd_d = TT(wlow, parm("w_dw", 31 * ND, 31 * NP_), wdh[:, :].bitcast(F32), ALU.subtract, wd_a, *arena_free)
        NDG = 16
        diag_t, diag_used, diag_next = {}, {}, [0]

        def diagonals(most=len(mtaps)):
            while diag_next[0] < most and (diag_next[0] < NDG or diag_next[0] - NDG in diag_used):
                n = diag_next[0]
                o = (slice(None), (n % NDG) // 2, slice(P * (n % 2), P * (n % 2) + P))
                diag_next[0] += 1
                m = 31 * mtaps[n][0] + mtaps[n][1]
                f = diag_used.get(n - NDG)
                a = A(yh[o], ident, ACT.Copy, wd_a, f, y_used[0], scale=wdh[:, m:m + 1].bitcast(F32))
                c = TS(yl[o], ident, wlow[:, m:m + 1], 1.0, ALU.mult, ALU.mult, wd_d, f, y_used[0], eng=pool)
                diag_t[n] = [a, c]

        def glu_evac(j):
            def f(t, b, tok):
                ga, gb = glu[:, t, 0:256], glu[:, t, 256:512]
                bias = bp1[:, 512 * j:512 * j + 512]
                d = STT(glu[:, t, :], ps[b][:, :], rstd[:, t:t + 1], bias, ALU.mult, ALU.add, tok, t_bp1,
                        rstd_ready[t])
                free[b] = rstd_used[t] = d
                a = A(gb, gb, ACT.Sigmoid, d)
                gl_done[j, t] = TT(u2[:, j % 2, t, :], ga, gb, ALU.mult, a, gl_read.get((j - 2, t)))
            return f

        def glu_turn(j):
            b = tbank()
            for t in range(2):
                for k in range(2):
                    tok = tr(ps[b][:, 256 * k + P * t:256 * k + P * t + P], u2[:, j % 2, t, P * k:P * k + P],
                             (gl_done[j, t], free[b]), inc=k == 1)
                gl_read[j, t] = tok
            a = A(upad[:, 2 * j:2 * j + 2, 30:286], ps[b][:, :].rearrange("p (k c) -> p k c", k=2), ACT.Copy, tok, z0)
            free[b] = up_t[2 * j] = up_t[2 * j + 1] = a

        def taps(c, lo, hi, *deps):
            for w in range(lo, hi):
                if cvt[c] is None:
                    d = TS(cv[:, c, :], upad[:, c, w:w + 256], parm("w_dw", 31 * c + w), parm("b_dw", c), ALU.mult, ALU.add,
                           up_t[c], z0)
                else:
                    d = STT(cv[:, c, :], upad[:, c, w:w + 256], parm("w_dw", 31 * c + w), cv[:, c, :], ALU.mult,
                            ALU.add, cvt[c], *deps)
                cvt[c] = d

        vtaps = {c: list(range(KT if c == 3 else 0, 31)) for c in (0, 1, 2, 3, 7)}
        turns = [(0, 1)] * 31 + [(2, 3)] * 2 + [(2,)] * 2 + [(2, 7)] * 27 + [(7,)] * 4

        def some_taps(n):
            while n > 0 and turns and all(up_t[c] for c in turns[0]):
                for c in turns.pop(0):
                    w = vtaps[c].pop(0)
                    taps(c, w, w + 1)
                    n -= 1

        u_parts = [(two[:, 0, :], two[:, 1, :])] + [tuple(
            x[:, 0:4, :].rearrange("p k c -> p (k c)")[:, 286 * n:286 * n + 286] for x in (xh, xl)) for n in range(3)]
        u_t = [None] * NP_

        def parts(n, *freed):
            hi, lo = u_parts[n]
            a = A(hi, upad[:, MT[n], :], ACT.Copy, up_t[MT[n]], z0, *freed)
            u_t[n] = TT(lo, upad[:, MT[n], :], hi.bitcast(F32), ALU.subtract, a)

        for j in range(4):
            later(3, lambda j=j: diagonals(4 * j + 4))
            if j:
                later(2, lambda j=j: glu_turn(j - 1))
                if j == 3:
                    later(2, lambda: parts(0))
                for g in range(4):
                    later(g, lambda: some_taps(3))
            tokc = in_chunk(glu_evac(j), second=(lambda: norm(1, "mix1")) if j == 0 else None)
            if j == 0:
                for t in range(2):
                    for half in range(2):
                        cols = slice(512 * half, 512 * half + 512)
                        h_ready[t][half] = TT(h[:, t, cols], h[:, t, cols], bp2[:, cols], ALU.add, h_ready[t][half],
                                              t_bp2, x_ready[t], junk_used[0], eng=pool)
        x_used[0] = tokc
        parts(1, tokc)
        parts(2, tokc)

        cbi = [4, 5, 0, 3]
        for n, (c, w) in enumerate(mtaps):
            last = w == (KT if c == 0 else 31) - 1
            b = cbi[c]
            if w == 0:
                pe.wait(u_t[c], free[b])
            pe.wait(*diag_t[n])
            o = (slice(None), (n % NDG) // 2, slice(P * (n % 2), P * (n % 2) + P))
            u_h, u_l = (x[:, w:w + 256] for x in u_parts[c])
            diag_used[n] = mm3(ps[b][:, 0:256], yh[o], yl[o], u_h, u_l, w == 0, last, inc=True)
            diagonals()
            if n == 60:
                free[whole_3[0]] = cvt[3] = TT(cv[:, 3, :], ps[whole_3[0]][:, 0:256], cv[:, 3, :], ALU.add, whole_3[1],
                                               cvt[3])
                assert not vtaps[3]
            if n == 9:
                glu_turn(3)
                parts(3, tokc)
            if n % 2:
                some_taps(2)
            if last and c == 0:
                whole_3 = (b, diag_used[n])
            elif last:
                a = A(cv[:, ND + c, :], ps[b][:, 0:256], ACT.Identity, diag_used[n], bias=parm("b_dw", ND + c))
                free[b] = cvt[ND + c] = a
        some_taps(1000)
        assert not turns and not any(vtaps.values())
        y_used[0] = diag_used[len(mtaps) - 1]

        def tcols(t):
            return slice(P * t, P * t + P)

        pe.wait(free[1], free[2])
        sum_t, sq_t, rs_t = [None] * 2, [None] * 2, [None] * 2
        order = [0, 1, 4, 5, 2, 3, 6, 7]
        for t in range(2):
            for n, c in enumerate(order):
                sum_t[t] = mm(ps[1 + t][:, 0:P], const("ones"), cv[:, c, tcols(t)], start=n == 0, stop=n == 7,
                              deps=(cvt[c],), inc=n == 7)
        def centre(t):
            mub = mu[:, tcols(t)].unsqueeze(1).to_broadcast([P, 4, P])
            a = free[1 + t] = A(mu[:, tcols(t)], ps[1 + t][:, 0:P], ACT.Copy, sum_t[t], scale=1.0 / D)
            sq_t[t] = []
            for half in range(2):
                v = cv[:, 4 * half:4 * half + 4, tcols(t)]
                d = TT(v, v, mub, ALU.subtract, a)
                sq_t[t].append(A(sq[:, 4 * half:4 * half + 4, tcols(t)], v, ACT.Square, d))

        def squares(t):
            d = TT(sq[:, 0:4, tcols(t)], sq[:, 0:4, tcols(t)], sq[:, 4:8, tcols(t)], ALU.add, *sq_t[t])
            return TT(sq[:, 0:2, tcols(t)], sq[:, 0:2, tcols(t)], sq[:, 2:4, tcols(t)], ALU.add, d)

        def deviation(t, d):
            for c in range(2):
                tok = mm(ps[6 + t][:, 0:1], sq[:, c, tcols(t)], const("ones", 1), start=c == 0, stop=c == 1,
                         deps=(d, free[6 + t]), inc=c == 1)
            d = TS(st[:, 48 + t:49 + t], ps[6 + t][:, 0:1], 1.0 / D, EPS, ALU.mult, ALU.add, tok)
            free[6 + t] = d
            rs_t[t] = TT(st[:, 48 + t:49 + t], st[:, 48 + t:49 + t], nhalf[:, 0:1], ALU.pow, d, eng=pool)

        def spread(t):
            d = TS(dg[:, t, :], ident, st[:, 48 + t:49 + t], 1.0, ALU.mult, ALU.mult, rs_t[t])
            rs_t[t] = mm(ps[4 + t][:, 0:P], const("ones"), dg[:, t, :], deps=(d, free[4 + t]))

        acts = [[], []]
        done = [[], []]

        def activate(t):
            rsb = ps[4 + t][:, 0:P].unsqueeze(1).to_broadcast([P, 4, P])
            for g in range(2):
                v = cv[:, 4 * g:4 * g + 4, tcols(t)]
                d = TT(v, v, rsb, ALU.mult, rs_t[t])
                free[4 + t] = d
                for c in range(4 * g, 4 * g + 4):
                    a = A(cv[:, c, tcols(t)], cv[:, c, tcols(t)], ACT.Silu, d, scale=parm("ln_g", c),
                          bias=parm("ln_b", c))
                    if c % 2:
                        w = (slice(None), slice(c - 1, c + 1), tcols(t))
                        acts[t].append((w, A(yh[w], cv[w], ACT.Copy, a, y_used[0])))

        def remainders(t):
            for w, a in acts[t]:
                done[t].append(TT(yl[w], cv[w], yh[w].bitcast(F32), ALU.subtract, a, y_used[0]))

        centre(0)
        tok = squares(0)
        centre(1)
        tables("silu_and_others")
        deviation(0, tok)
        spread(0)
        activate(0)
        deviation(1, squares(1))
        remainders(0)
        us = take(2, 1)
        out_part(us[0], 0, 0, yh, yl, [done[0][0]] * 2, True, False)
        spread(1)
        activate(1)
        remainders(1)
        pump()
        out_part(us[1], 0, 2, yh, yl, [done[0][1]] * 2, False, False)
        for n in range(2):
            out_part(us[n], 1, 2 * n, yh, yl, [done[1][n]] * 2, n == 0, False)
        y_used[0] = out_last((4, 6), yh, yl, [[done[0][n], done[1][n]] for n in (2, 3)], None, "ffn1")

        arena_free = [y_used[0], list(free)]
        ffn("ffn1", 1.0, "n1")
        ffn("n1", 0.5, "nm")

        gb = ar(0, 2048)
        cosn = ar(2048, 2, 2, 128)
        rm = ar(2560, 4, 384)
        pm = ar(4096, 4, 384)
        t_gb = load(gb, brow["gate_bias"], *arena_free)
        t_cs = load(cosn.rearrange("p a b c -> p (a b c)"), cosin)
        t_rm = load(rm.rearrange("p a b -> p (a b)"), rmask)
        t_pm = load(pm.rearrange("p a b -> p (a b)"), pmat)
        merged = ar(5632, 2, D)
        qT = ar(7680, 4, T)
        kT = ar(8704, 4, T)
        sig0 = ar(7680, 2, D)
        vn = ar(9728, 2, 1024)
        pn = ar(9728, 2, 1024)
        ro = ar(11776, 2, 512)
        sc = [ar(12800, 384), ar(13696, 384)]
        gt = ar(13184, 512)
        rtmp = ar(13184, 256)

        p_t = [[None, None], [None, None]]

        def p_evac(j):
            def f(t, b, tok):
                free[b] = p_t[j][t] = A(pn[:, t, 512 * j:512 * j + 512], ps[b][:, :], ACT.Copy, tok, rstd_ready[t],
                                        scale=rstd[:, t:t + 1])
            return f

        pl_ready, pn_read = {}, [None]

        def pooled(g):
            b = tbank()
            pe.wait(free[b], *p_t[g // 2], t_pm)
            for c in (2 * g, 2 * g + 1):
                o = 256 * (c % 2)
                cols = slice(P * c, P * c + P)
                mm(ps[b][:, o:o + 256], pn[:, 0, cols], pm[:, g, 0:256], start=c % 2 == 0, stop=False, skip=True,
                   inc=False)
                tok = mm(ps[b][:, o + 128:o + 256], pn[:, 1, cols], pm[:, g, 256:384], start=False, stop=True,
                         skip=True)
            src = ps[b][:, :].rearrange("p (k c) -> p k c", k=2)
            a = A(yh[:, 2 * g:2 * g + 2, :], src, ACT.Copy, tok, y_used[0])
            d = TT(yl[:, 2 * g:2 * g + 2, :], src, yh[:, 2 * g:2 * g + 2, :].bitcast(F32), ALU.subtract, a)
            free[b] = pl_ready[g] = d
            pn_read[0] = tok

        sg_t = {}

        def gate_evac(which, j, dst, *freed):
            def f(t, b, tok):
                g_ = dst[:, t, 512 * j:512 * j + 512]
                d = STT(g_, ps[b][:, :], rstd[:, t:t + 1], gb[:, 1024 * which + 512 * j:1024 * which + 512 * j + 512],
                        ALU.mult, ALU.add, tok, rstd_ready[t], t_gb, *freed)
                free[b] = rstd_used[t] = d
                sg_t[(which, j, t)] = A(g_, g_, ACT.Sigmoid, d)
            return f

        mg_t = {}

        def pool_evac(j):
            def f(t, b, tok):
                m = merged[:, t, 512 * j:512 * j + 512]
                free[b] = mg_t[(j, t)] = TT(m, ps[b][:, :], m, ALU.mult, tok, sg_t[(1, j, t)])
            return f

        def merge_evac(j):
            def f(t, b, tok):
                m = merged[:, t, 512 * j:512 * j + 512]
                s_ = sig0[:, t, 512 * j:512 * j + 512]
                d = free[b] = TT(s_, ps[b][:, :], s_, ALU.mult, tok, sg_t[(0, j, t)])
                mg_t[(j, t)] = TT(m, m, s_, ALU.add, d, mg_t[(j, t)])
            return f

        for j in range(2):
            in_chunk(p_evac(j), second=(lambda: norm(1, "nm")) if j == 0 else None)
        later(0, lambda: pooled(0))
        later(1, lambda: pooled(1))
        later(2, lambda: pooled(2))
        later(3, lambda: pooled(3))
        for j in range(2):
            in_chunk(gate_evac(1, j, merged))
        u, = take(1)
        pe.wait(lo_done[u])
        for g in range(4):
            pe.wait(free[g], pl_ready[g])
            for dd in range(2):
                for cc in range(2):
                    c = 512 * g + 256 * cc + P * dd
                    tok = mm3(ps[g][:, 256 * dd:256 * dd + 256], whi[:, u % S, c:c + P], wlo[:, u % S, c:c + P],
                              yh[:, 2 * g + cc, :], yl[:, 2 * g + cc, :], cc == 0, cc == 1, inc=cc == 1)
            pl_ready[g] = tok
        unit_done[u] = tok
        pool_ready = []
        for g in range(4):
            for k in (2 * g, 2 * g + 1):
                a = A(yh[:, k, :], ps[g][:, 256 * (k % 2):256 * (k % 2) + 256], ACT.Copy, pl_ready[g],
                      scale=parm("pool", k))
            for k in (2 * g, 2 * g + 1):
                d = STT(yl[:, k, :], ps[g][:, 256 * (k % 2):256 * (k % 2) + 256], parm("pool", k),
                        yh[:, k, :].bitcast(F32), ALU.mult, ALU.subtract, a)
            free[g] = d
            pool_ready.append(d)
        pool_r = [[pool_ready[1], pool_ready[3]]] * 2

        ro_read, rt_read, tr_read = [None, None], [None], [None]
        v_t = [[None, None], [None, None]]

        def v_evac(j):
            def f(t, b, tok):
                free[b] = v_t[j][t] = A(vn[:, t, 512 * j:512 * j + 512], ps[b][:, :], ACT.Copy, tok, rstd_ready[t],
                                        pn_read[0], scale=rstd[:, t:t + 1])
            return f

        def rot_evac(dst, ready):
            def f(t, b, tok):
                x = ps[b][:, :].rearrange("p (h a d) -> p h a d", h=2, a=2)
                o = ro[:, t, :].rearrange("p (h a d) -> p h a d", h=2, a=2)
                w = rtmp[:, :].rearrange("p (h d) -> p h d", h=2)
                cs_, sn = (cosn[:, t, i:i + 1, :].to_broadcast([P, 2, 128]) for i in range(2))
                r_ = rstd[:, t:t + 1]
                d1 = STT(o[:, :, 0, :], x[:, :, 0, :], r_, cs_, ALU.mult, ALU.mult, tok, rstd_ready[t], t_cs,
                         ro_read[t])
                d2 = STT(w, x[:, :, 1, :], r_, sn, ALU.mult, ALU.mult, rt_read[0])
                d1 = TT(o[:, :, 0, :], o[:, :, 0, :], w, ALU.subtract, d1, d2)
                d2 = STT(w, x[:, :, 0, :], r_, sn, ALU.mult, ALU.mult, d1)
                d3 = STT(o[:, :, 1, :], x[:, :, 1, :], r_, cs_, ALU.mult, ALU.mult)
                free[b] = d3
                d = TT(o[:, :, 1, :], o[:, :, 1, :], w, ALU.add, d3)
                rt_read[0] = d

                def turned():
                    b2 = tbank()
                    for i in range(4):
                        tk = tr(ps[b2][:, P * i:P * i + P], ro[:, t, P * i:P * i + P], (d, free[b2]), inc=i == 3)
                    ro_read[t] = tk
                    free[b2] = ready[t] = A(dst[:, :, P * t:P * t + P],
                                            ps[b2][:, :].rearrange("p (k c) -> p k c", k=4), ACT.Copy, tk,
                                            tr_read[0])
                later(2, turned)
            return f

        sc_t, pv_t = {}, {}
        ret_t = {}

        def ret_scores(i, q_r, k_r):
            hh = 2 * (i % 2)
            sb_ = i % 2
            pe.wait(free[sb_], *q_r, *k_r)
            for c in range(2):
                mm(ps[sb_][:, 0:256], kT[:, hh + c, 0:128], qT[:, hh + c, :], start=c == 0, stop=c == 1, inc=False)
            for c in range(2):
                tok = mm(ps[sb_][:, 256:384], kT[:, hh + c, 128:256], qT[:, hh + c, 128:256], start=c == 0,
                         stop=c == 1, inc=c == 1)
            tr_read[0] = tok
            d = TT(sc[sb_], ps[sb_][:, 0:384], rm[:, i, :], ALU.mult, tok, t_rm, pv_t.get(i - 2))
            free[sb_] = sc_t[i] = d

        def ret_values(i):
            vc = slice(256 * i, 256 * i + 256)
            s_ = sc[i % 2]
            pe.wait(sc_t[i], free[2], free[3], *v_t[i // 2])
            c0 = 256 * (i % 2)
            mm(ps[2][:, c0:c0 + 256], s_[:, 0:128], vn[:, 0, vc], inc=False)
            mm(ps[3][:, c0:c0 + 256], s_[:, 128:256], vn[:, 0, vc], start=True, stop=False, inc=False)
            pv_t[i] = mm(ps[3][:, c0:c0 + 256], s_[:, 256:384], vn[:, 1, vc], start=False, stop=True)

        def ret_norm(j):
            for t in range(2):
                v_ = vn[:, t, 512 * j:512 * j + 512]
                v3 = v_.rearrange("p (h d) -> p h d", h=2)
                a = A(v_, ps[2 + t][:, :], ACT.Copy, pv_t[2 * j + 1])
                free[2 + t] = a
                s2 = st[:, 50 + 4 * j + 2 * t:52 + 4 * j + 2 * t]
                r_ = (sil, hid)[t][:, :, :].rearrange("p a c -> p (a c)")
                d = TT(r_, v_, v_, ALU.mult, a)
                d = dve.do(lambda e, s2=s2, r3=r_.rearrange("p (h d) -> p h d", h=2): e.tensor_reduce(
                    s2, r3, AXX, ALU.add), d)
                d = rsqrt(s2, s2, 256, d)
                ret_t[(j, t)] = TT(v3, v3, s2.unsqueeze(2).to_broadcast([P, 2, 256]), ALU.mult, d)

        gt_read = [None]
        gs_t = {}

        def gret_evac(j):
            def f(t, b, tok):
                a = A(gt, ps[b][:, :], ACT.Silu, tok, rstd_ready[t], gt_read[0], rt_read[0], scale=rstd[:, t:t + 1])
                free[b] = a
                v_ = vn[:, t, 512 * j:512 * j + 512]
                gt_read[0] = gs_t[(j, t)] = TT(v_, v_, gt, ALU.mult, a, ret_t[(j, t)])
            return f

        def ret_turn(t, half):
            y_ready[t][half] = xpose_half(vn[:, t, :], t, half, yh, yl, lambda k: None, gs_t[(half, t)], y_used[0])

        in_chunk(v_evac(0))
        in_chunk(pool_evac(0), banks=(0, 1), lhs=(yh, yl, pool_r))
        y_used[0] = in_chunk(pool_evac(1), banks=(0, 1), lhs=(yh, yl, pool_r))
        in_chunk(v_evac(1))
        q_r, k_r = [None, None], [None, None]
        in_chunk(rot_evac(qT, q_r))
        in_chunk(rot_evac(kT, k_r))
        later(2, lambda: (ret_scores(0, q_r, k_r), ret_scores(1, q_r, k_r)))
        later(3, lambda: (ret_values(0), ret_values(1), ret_norm(0)))
        q_r2, k_r2 = [None, None], [None, None]
        in_chunk(rot_evac(qT, q_r2))
        in_chunk(rot_evac(kT, k_r2))
        later(2, lambda: (ret_scores(2, q_r2, k_r2), ret_scores(3, q_r2, k_r2)))
        later(3, lambda: (ret_values(2), ret_values(3), ret_norm(1)))
        in_chunk(gret_evac(0))
        y_ready = [[None, None], [None, None]]
        later(1, lambda: ret_turn(0, 0))
        later(2, lambda: ret_turn(1, 0))
        in_chunk(gret_evac(1))
        later(1, lambda: ret_turn(0, 1))
        later(2, lambda: ret_turn(1, 1))
        in_chunk(gate_evac(0, 0, sig0, tr_read[0]))
        x_used[0] = in_chunk(gate_evac(0, 1, sig0))
        in_chunk(merge_evac(0), banks=(0, 1), lhs=(yh, yl, y_ready))
        z_ready = [[None, None], [None, None]]

        def merged_turn(t, half):
            z_ready[t][half] = xpose_half(merged[:, t, :], t, half, xh, xl, lambda k: None, mg_t[(half, t)],
                                          x_used[0])

        later(1, lambda: merged_turn(0, 0))
        later(3, lambda: merged_turn(1, 0))
        y_used[0] = in_chunk(merge_evac(1), banks=(0, 1), lhs=(yh, yl, y_ready))
        us = take(2)
        for n in range(2):
            for t in range(2):
                out_part(us[n], t, 2 * n, xh, xl, [z_ready[0][0], z_ready[1][0]], n == 0, False)
            if n == 0:
                merged_turn(0, 1)
                merged_turn(1, 1)
        zr1 = [z_ready[0][1], z_ready[1][1]]
        x_held = x_used[0]
        us = take(2)
        for n in range(2):
            tok = out_part(us[n], 0, 4 + 2 * n, xh, xl, zr1, False, n == 1)
        residual(0, tok)
        out_part(us[0], 1, 4, xh, xl, zr1, False, False)
        x_used[0] = tok
        norm(0, "n2")
        tok = out_part(us[1], 1, 6, xh, xl, zr1, False, True)
        x_used[0] = tok
        residual(1, tok)
        arena_free = [tok, list(free)]
        ffn("n2", 0.5, None)

        fin = ar(0, 1024)
        t_f = load(fin, brow["norm_final"], *arena_free)
        res = ar(1024, 2, D)
        stores = []
        for t in range(2):
            a = A(junk, h[:, t, :], ACT.Square, *h_ready[t], junk_used[0], accum=ss[:, t:t + 1])
            junk_used[0] = a
            d = rsqrt(rstd[:, t:t + 1], ss[:, t:t + 1], D, a, rstd_used[t])
            d = STT(res[:, t, :], h[:, t, :], rstd[:, t:t + 1], fin, ALU.mult, ALU.mult, d, t_f, arena_free)
            sem = ctx.enter_context(nc.semaphore(f"stored{t}"))
            sp.wait(d)
            sp.items.append(lambda e, t=t, sem=sem: e.dma_start(out[t], res[:, t, :]).then_inc(sem, 16))
            stores.append((sem, 16))
        sp.wait(*stores)
        assert at[0] == NU

        block = ctx.enter_context(nc.Block())

        @block.sync
        def _(e):
            for f in sp.items:
                f(e)

        @block.tensor
        def _(e):
            for f in pe.items:
                f(e)

        @block.scalar
        def _(e):
            for f in act.items:
                f(e)

        @block.vector
        def _(e):
            for f in dve.items:
                f(e)

        @block.gpsimd
        def _(e):
            for f in pool.items:
                f(e)


def constants():
    import numpy as np
    i = np.arange(128)
    cst = np.zeros((128, NKW), np.float32)
    cst[:, 0:128] = np.eye(128)
    cst[:, 128:256] = i[:, None] > i[None, :]
    cst[:, 256:384] = 1
    cst[:, 384:512] = cst[:, 512:640] = i[:, None] < i[None, :]
    cst[:, 640:768] = (i[:, None] > i[None, :]) & (i[:, None] // 64 == i[None, :] // 64)
    cst[:, 768:770] = i[:, None] // 64 == np.arange(2)[None, :]
    half = 128
    inv = (np.float32(10000.0) ** (-np.arange(half, dtype=np.float32) / np.float32(half))).astype(np.float32)
    ang = np.arange(256, dtype=np.float32)[:, None] * inv[None, :]
    cs = np.stack([np.cos(ang), np.sin(ang)], axis=1).astype(np.float32)
    cosin = np.ascontiguousarray(cs.reshape(2, 128, 2, 128).transpose(1, 0, 2, 3).reshape(128, 512))
    s = np.arange(256)
    rmask = np.zeros((128, 4, 384), np.float32)
    for g in range(4):
        gamma = 1.0 - 2.0 ** (-5.0 - g)
        m = np.where(s[:, None] // 64 <= s[None, :] // 64, gamma ** np.abs(s[:, None] - s[None, :]), 0.0) / 16.0
        rmask[:, g, 0:256] = m[0:128]
        rmask[:, g, 256:384] = m[128:256, 128:256]
    pmat = np.zeros((128, 4, 384), np.float32)
    for g, w in enumerate((2, 4, 8, 16)):
        d = s[None, :] - s[:, None]
        m = ((d >= 0) & (d < w)) / np.minimum(s[None, :] + 1.0, w) - (d == 0)
        pmat[:, g, 0:256] = m[0:128]
        pmat[:, g, 256:384] = m[128:256, 128:256]
    return cst, cosin, rmask.reshape(128, -1), pmat.reshape(128, -1)


def units_in(w):
    n = w.shape[1] // 512
    return w.reshape(2, 4, 128, n, 512).transpose(3, 0, 2, 1, 4).reshape(2 * n, 128, 2048)


def units_out(w):
    n = w.shape[0] // 256
    return w.reshape(n, 2, 128, 1024).transpose(0, 2, 1, 3).reshape(n, 128, 2048)


def units_ffn(wg, wu, wd):
    import numpy as np
    pair = np.stack([wg.reshape(1024, FC, 256), wu.reshape(1024, FC, 256)], axis=2).reshape(1024, FC * 512)
    a, b = units_in(pair), units_out(wd)
    seq = [a[0], a[1]]
    for j in range(1, FC - 2):
        seq += [a[2 * j], a[2 * j + 1], b[j - 1]]
    return seq + [*a[2 * FC - 4:], *b[FC - 3:]]


def layout(i):
    import numpy as np
    cst, cosin, rmask, pmat = constants()
    win = i["hy_w_in"][0]
    col = {}
    c = 0
    for n, w in (("gq", 256), ("gk", 256), ("gv", 512), ("gr", 512), ("glr", 16), ("sq", 512), ("sk", 512),
                 ("sv", 512)):
        col[n] = win[:, c:c + w]
        c += w
    seq = []
    for n in ("sq", "sk", "sv"):
        seq += list(units_in(col[n]))
    seq += list(units_in(np.concatenate([col["gq"], col["gk"]], axis=1)))
    seq += list(units_in(col["gv"])) + list(units_in(col["gr"]))
    ho = units_out(i["hy_w_out"][0])
    seq += [*ho[2:4], *ho[0:2]]
    seq += units_ffn(i["ffn_w_gate"][0], i["ffn_w_up"][0], i["ffn_w_down"][0])
    pw = i["cv_w_pw1"][0].reshape(1024, 2, 4, 256).transpose(0, 2, 1, 3).reshape(1024, 2048)
    seq += list(units_in(pw)) + list(units_out(i["cv_w_pw2"][0]))
    seq += units_ffn(i["ffn_w_gate"][1], i["ffn_w_up"][1], i["ffn_w_down"][1])
    f1 = i["ffn1_w_in_2"][0]
    seq += units_ffn(f1[:, :2816], f1[:, 2816:], i["ffn1_w_out_2"][0])
    w2 = i["w_in_2"][0]
    q, k, v, g, p = (w2[:, 1024 * n:1024 * n + 1024] for n in range(5))
    g0, g1 = w2[:, 5120:6144], w2[:, 6144:7168]
    v_ = units_in(v)
    seq += [*units_in(p), *units_in(g1)]
    seq.append(i["pool_w_2"][0].reshape(4, 2, 128, 256).transpose(2, 0, 1, 3).reshape(128, 2048))
    seq += [*v_[0:2], *units_in(i["w_pool_up_2"][0]), *v_[2:4]]
    a, b = units_in(q), units_in(k)
    seq += [*a[0:2], *b[0:2], *a[2:4], *b[2:4]]
    seq += [*units_in(g), *units_in(g0), *units_in(i["w_ret_up_2"][0])]
    seq += list(units_out(i["w_out_2"][0]))
    f2 = i["ffn2_w_in_2"][0]
    seq += units_ffn(f2[:, :2816], f2[:, 2816:], i["ffn2_w_out_2"][0])

    def cols(x):
        return x.reshape(-1, 128).T

    def twice(x):
        return np.concatenate([x, x]).reshape(128, 1)

    par = np.concatenate([
        cols(i["mix_norm"][0]), cols(i["ffn_norm"][0]), cols(i["mix_norm"][1]), cols(i["ffn_norm"][1]),
        cols(i["norm_ffn1_2"][0]), cols(i["norm_mix_2"][0]), cols(i["norm_ffn2_2"][0]), cols(i["hy_gla_norm"][0]),
        twice(i["hy_sb_q_norm"][0]), twice(i["hy_sb_k_norm"][0]), cols(i["cv_b_dw"][0]), cols(i["cv_ln_g"][0]),
        cols(i["cv_ln_b"][0]), cols(i["pool_scale_2"][0]),
        i["cv_w_dw"][0].reshape(31, 8, 128).transpose(2, 1, 0).reshape(128, 248)], axis=1)

    def rows(x):
        return np.broadcast_to(x.reshape(1, -1), (128, x.size))

    return {
        "x": i["x"].reshape(2, 128, 1024), "w": np.stack(seq),
        "wg": col["glr"].reshape(8, 128, 16).transpose(1, 0, 2).reshape(128, 128), "wg2": i["hy_w_gate2"][0],
        "cst": cst, "par": par, "b_gate": rows(i["hy_b_gate"][0]),
        "b_pw1": rows(i["cv_b_pw1"][0].reshape(2, 4, 256).transpose(1, 0, 2)),
        "b_pw2": rows(i["cv_b_pw2"][0]), "gate_bias": rows(i["gate_bias_2"][0]),
        "norm_final": rows(i["norm_final_2"]), "cosin": cosin, "rmask": rmask, "pmat": pmat,
    }


def kernel(**inputs):
    import numpy as np
    import concourse.bacc as bacc
    from concourse.bass_utils import run_bass_kernel_spmd
    laid = layout({k: np.asarray(v) for k, v in inputs.items()})
    nc = bacc.Bacc("TRN2", target_bir_lowering=False, num_devices=1)
    arrays, aps = {}, {}
    for name, a in laid.items():
        a = np.ascontiguousarray(a)
        arrays["in_" + name] = a
        aps[name] = nc.dram_tensor("in_" + name, a.shape, mybir.dt.from_np(a.dtype), kind="ExternalInput").ap()
    out = nc.dram_tensor("out_0", (2, 128, 1024), F32, kind="ExternalOutput").ap()
    build(nc, aps["x"], aps["w"], aps["wg"], aps["wg2"], aps["cst"], aps["par"],
          {n: aps[n] for n in ("b_gate", "b_pw1", "b_pw2", "gate_bias", "norm_final")}, aps["cosin"], aps["rmask"],
          aps["pmat"], out)
    r = run_bass_kernel_spmd(nc, [arrays], core_ids=[0])
    return r.results[0]["out_0"].reshape(1, 256, 1024)
```
